# Optimizing a Trainium2 kernel written in Bass

```python
import jax, jax.numpy as jnp
from jax import lax
import numpy as np
import jax
import jax.numpy as jnp

D_MODEL = 1024
BATCH = 1
SEQ = 256
DEPTH = 2

CHUNK = 64
D_MIX = D_MODEL
GM_WIDTH = D_MIX // 2
GM_HEADS = 8
GM_HEAD_DIM = GM_WIDTH // GM_HEADS
GM_BLOCK = 128
SB_WIDTH = D_MIX - GM_WIDTH
SB_HEADS = 8
SB_HEAD_DIM = SB_WIDTH // SB_HEADS
SB_BLOCK = 128
IN_COLS = 2 * GM_WIDTH + 3 * SB_WIDTH
PEER_HEADS = 8
PEER_QUERY_DIM = 256
PEER_HALF = PEER_QUERY_DIM // 2
N_KEYS = 128
N_EXPERTS = N_KEYS * N_KEYS
PEER_TOPK = 16
PEER_BLOCK = 128
ADA_SCALE = 0.5
EPS = 1e-6


def rmsnorm(x, g):
    xf = x.astype(jnp.float32)
    y = xf * lax.rsqrt(jnp.mean(xf * xf, axis=-1, keepdims=True) + EPS)
    return (y * g.astype(jnp.float32)).astype(x.dtype)

def spatial_gating(u, v, ws, bs, v_gain):
    B, S, _ = v.shape
    pos_chunk = jnp.arange(GM_BLOCK) // CHUNK
    mask = pos_chunk[None, :] <= pos_chunk[:, None]
    w = jnp.where(mask[None], ws, jnp.zeros_like(ws))
    vh = v.reshape(B, S // GM_BLOCK, GM_BLOCK, GM_HEADS, GM_HEAD_DIM)
    vh = rmsnorm(vh, v_gain.reshape(GM_HEADS, GM_HEAD_DIM))
    z = jnp.einsum('hts,bnshc->bnthc', w, vh) + bs.T[None, None, :, :, None]
    return u * z.reshape(B, S, GM_WIDTH)

def stick_breaking(q, k, v):
    B, S, H, dh = q.shape
    scale = 1.0 / np.sqrt(dh)
    outs = []
    for i in range(S // SB_BLOCK):
        t0, t1 = i * SB_BLOCK, (i + 1) * SB_BLOCK
        qb, kb, vb = q[:, t0:t1], k[:, :t1], v[:, :t1]
        z = jnp.einsum('bthd,bshd->bhts', qb, kb).astype(jnp.float32) * scale
        t_idx = t0 + jnp.arange(SB_BLOCK)[:, None]
        s_idx = jnp.arange(t1)[None, :]
        causal = s_idx < t_idx
        log_beta = jax.nn.log_sigmoid(z)
        log_keep = jnp.where(causal, jax.nn.log_sigmoid(-z), 0.0)
        later = lax.cumsum(log_keep, axis=3, reverse=True) - log_keep
        a = jnp.where(causal, jnp.exp(log_beta + later), 0.0)
        outs.append(jnp.einsum('bhts,bshd->bthd', a.astype(vb.dtype), vb))
    return jnp.concatenate(outs, axis=1)

def mixer(h, w_in, gm_ws, gm_bs, gm_vnorm, out_norm_a, out_norm_b, w_out):
    B, S, _ = h.shape
    proj = h @ w_in
    a_u, a_v, sq, sk, sv = jnp.split(
        proj, [GM_WIDTH, 2 * GM_WIDTH, 2 * GM_WIDTH + SB_WIDTH, 2 * GM_WIDTH + 2 * SB_WIDTH], axis=-1)
    y_a = spatial_gating(jax.nn.gelu(a_u), jax.nn.gelu(a_v), gm_ws, gm_bs, gm_vnorm)
    hs = (B, S, SB_HEADS, SB_HEAD_DIM)
    y_b = stick_breaking(sq.reshape(hs), sk.reshape(hs), sv.reshape(hs)).reshape(B, S, SB_WIDTH)
    y = jnp.concatenate([rmsnorm(y_a, out_norm_a), rmsnorm(y_b, out_norm_b)], axis=-1)
    return y @ w_out

def peer_ffn(h, wq, k1, k2, u_tab, v_tab):
    B, S, D = h.shape
    hb = h.reshape((B * S) // PEER_BLOCK, PEER_BLOCK, D)

    def block(xb):
        q = (xb @ wq).reshape(PEER_BLOCK, PEER_HEADS, 2, PEER_HALF)
        s1 = jnp.einsum('phd,kd->phk', q[:, :, 0], k1).astype(jnp.float32)
        s2 = jnp.einsum('phd,kd->phk', q[:, :, 1], k2).astype(jnp.float32)
        v1, i1 = lax.top_k(s1, PEER_TOPK)
        v2, i2 = lax.top_k(s2, PEER_TOPK)
        cand = (v1[..., :, None] + v2[..., None, :]).reshape(PEER_BLOCK, PEER_HEADS, PEER_TOPK * PEER_TOPK)
        cand_id = (i1[..., :, None] * N_KEYS + i2[..., None, :]).reshape(PEER_BLOCK, PEER_HEADS, PEER_TOPK * PEER_TOPK)
        top_s, top_pos = lax.top_k(cand, PEER_TOPK)
        eid = jnp.take_along_axis(cand_id, top_pos, axis=-1)
        g = jax.nn.softmax(top_s, axis=-1)
        ue = u_tab[eid]
        ve = v_tab[eid]
        act = jax.nn.gelu(jnp.einsum('pd,phkd->phk', xb, ue))
        return jnp.einsum('phk,phkd->pd', g.astype(xb.dtype) * act, ve)

    return lax.map(block, hb).reshape(B, S, D)

def first_inputs(seed: int = 0) -> dict:
    key = jax.random.key(seed)
    ks = jax.random.split(key, 20)
    f32 = jnp.float32
    nrm = lambda k, shape, s: jax.random.normal(k, shape, f32) * s
    L, D = DEPTH, D_MODEL
    return {
        "x": nrm(ks[0], (BATCH, SEQ, D), 1.0),
        "c": nrm(ks[1], (BATCH, D), 1.0),
        "ada_w": nrm(ks[2], (L, D, 6 * D), ADA_SCALE * D ** -0.5),
        "ada_b": nrm(ks[3], (L, 6 * D), 0.02),
        "norm_mix": 1.0 + nrm(ks[4], (L, D), 0.05),
        "norm_ffn": 1.0 + nrm(ks[5], (L, D), 0.05),
        "w_in": nrm(ks[6], (L, D, IN_COLS), D ** -0.5),
        "gm_ws": nrm(ks[7], (L, GM_HEADS, GM_BLOCK, GM_BLOCK), GM_BLOCK ** -0.5),
        "gm_bs": 1.0 + nrm(ks[8], (L, GM_HEADS, GM_BLOCK), 0.1),
        "gm_vnorm": 1.0 + nrm(ks[9], (L, GM_WIDTH), 0.05),
        "out_norm_a": 1.0 + nrm(ks[10], (L, GM_WIDTH), 0.05),
        "out_norm_b": 1.0 + nrm(ks[11], (L, SB_WIDTH), 0.05),
        "w_out": nrm(ks[12], (L, D_MIX, D), D_MIX ** -0.5),
        "peer_wq": nrm(ks[13], (L, D, PEER_HEADS * PEER_QUERY_DIM), D ** -0.5),
        "peer_k1": nrm(ks[14], (L, N_KEYS, PEER_HALF), PEER_HALF ** -0.5),
        "peer_k2": nrm(ks[15], (L, N_KEYS, PEER_HALF), PEER_HALF ** -0.5),
        "peer_u": nrm(ks[16], (L, N_EXPERTS, D), D ** -0.5),
        "peer_v": nrm(ks[17], (L, N_EXPERTS, D), PEER_HEADS ** -0.5),
        "final_norm": 1.0 + nrm(ks[18], (D,), 0.05),
    }

def first_block(x, c, ada_w, ada_b, norm_mix, norm_ffn, w_in, gm_ws, gm_bs, gm_vnorm,
              out_norm_a, out_norm_b, w_out, peer_wq, peer_k1, peer_k2, peer_u, peer_v,
              final_norm):
    c_act = jax.nn.silu(c)
    for l in range(DEPTH):
        mod = c_act @ ada_w[l] + ada_b[l]
        sh1, sc1, g1, sh2, sc2, g2 = jnp.split(mod[:, None, :], 6, axis=-1)
        h = rmsnorm(x, norm_mix[l]) * (1.0 + sc1) + sh1
        x = x + g1 * mixer(h, w_in[l], gm_ws[l], gm_bs[l], gm_vnorm[l],
                           out_norm_a[l], out_norm_b[l], w_out[l])
        h = rmsnorm(x, norm_ffn[l]) * (1.0 + sc2) + sh2
        x = x + g2 * peer_ffn(h, peer_wq[l], peer_k1[l], peer_k2[l], peer_u[l], peer_v[l])
    return rmsnorm(x, final_norm)


RMS_EPS = 1e-6
SSD_WIDTH = D_MODEL
SSD_HEAD_DIM = 64
SSD_HEADS = SSD_WIDTH // SSD_HEAD_DIM
SSD_GROUPS = 2
SSD_HEADS_PER_GROUP = SSD_HEADS // SSD_GROUPS
SSD_STATE = 64
SSD_CONV = 4
SSD_CHUNK = 128
SSD_CONV_DIM = SSD_WIDTH + 2 * SSD_GROUPS * SSD_STATE
GLA_HEADS = 8
GLA_VALUE_WIDTH = D_MODEL
GLA_KEY_WIDTH = D_MODEL // 2
GLA_HEAD_K = GLA_KEY_WIDTH // GLA_HEADS
GLA_HEAD_V = GLA_VALUE_WIDTH // GLA_HEADS
GLA_GATE_RANK = 16
GLA_GATE_NORMALIZER = 16.0
GLA_CHUNK = 64
EVEN_SPLITS = (SSD_WIDTH, SSD_CONV_DIM, SSD_HEADS, GLA_KEY_WIDTH, GLA_KEY_WIDTH, GLA_VALUE_WIDTH, GLA_GATE_RANK, GLA_VALUE_WIDTH)
EVEN_IN_WIDTH = sum(EVEN_SPLITS)
EVEN_MIX_WIDTH = SSD_WIDTH + GLA_VALUE_WIDTH
MOBA_HEADS = 16
MOBA_HEAD_DIM = 64
MOBA_WIDTH = MOBA_HEADS * MOBA_HEAD_DIM
MOBA_BLOCK = 256
MOBA_TOPK = 3
MOBA_Q_CHUNK = 32
ODD_IN_WIDTH = 4 * MOBA_WIDTH
N_EVEN = (DEPTH + 1) // 2
N_ODD = DEPTH // 2


def rms_norm(x, w):
    x32 = x.astype(jnp.float32)
    y = x32 * lax.rsqrt(jnp.mean(x32 * x32, axis=-1, keepdims=True) + RMS_EPS)
    return y * w.astype(jnp.float32)

def split_cols(u, sizes):
    cuts = [int(c) for c in np.cumsum(sizes)[:-1]]
    return jnp.split(u, cuts, axis=-1)

def causal_depthwise_conv(u, w, b):
    k_width = w.shape[0]
    y = lax.conv_general_dilated(u, w.astype(u.dtype)[:, None, :], window_strides=(1,), padding=[(k_width - 1, 0)], dimension_numbers=('NWC', 'WIO', 'NWC'), feature_group_count=u.shape[-1])
    return y + b.astype(u.dtype)

def ssd_chunked_scan(xs, dt, a, bm, cm, d_skip):
    b, L, G, E, P = xs.shape
    N = bm.shape[-1]
    Q = SSD_CHUNK
    nc = L // Q
    x_c = xs.reshape(b, nc, Q, G, E, P)
    dt_c = dt.reshape(b, nc, Q, G, E)
    xdt = x_c * dt_c[..., None]
    b_c = bm.reshape(b, nc, Q, G, N)
    c_c = cm.reshape(b, nc, Q, G, N)
    a_cs = jnp.cumsum(dt_c * a, axis=2)
    a_t = jnp.moveaxis(a_cs, 2, -1)
    seg = a_t[..., :, None] - a_t[..., None, :]
    causal = jnp.tril(jnp.ones((Q, Q), dtype=bool))
    decay_ij = jnp.exp(jnp.where(causal, seg, -jnp.inf))
    cb = jnp.einsum('bcign,bcjgn->bcgij', c_c, b_c)
    y_diag = jnp.einsum('bcgeij,bcjgep->bcigep', cb[:, :, :, None] * decay_ij, xdt)
    a_last = a_cs[:, :, -1]
    decay_to_end = jnp.exp(a_last[:, :, None] - a_cs)
    chunk_states = jnp.einsum('bcjgn,bcjge,bcjgep->bcgepn', b_c, decay_to_end, xdt)

    def carry_state(h, inp):
        chunk_decay, s = inp
        return chunk_decay[..., None, None] * h + s, h

    _, prev_states = lax.scan(carry_state, jnp.zeros_like(chunk_states[:, 0]), (jnp.moveaxis(jnp.exp(a_last), 1, 0), jnp.moveaxis(chunk_states, 1, 0)))
    prev_states = jnp.moveaxis(prev_states, 0, 1)
    y_off = jnp.einsum('bcign,bcgepn->bcigep', c_c, prev_states) * jnp.exp(a_cs)[..., None]
    y = y_diag + y_off + d_skip[:, :, None] * x_c
    return y.reshape(b, L, G * E * P)

def gla_chunked(q, k, v, log_decay):
    b, L, H, dk = q.shape
    dv = v.shape[-1]
    C = GLA_CHUNK
    n = L // C
    q = q.reshape(b, n, C, H, dk)
    k = k.reshape(b, n, C, H, dk)
    v = v.reshape(b, n, C, H, dv)
    gcs = jnp.cumsum(log_decay.reshape(b, n, C, H, dk), axis=2)
    ref = gcs[:, :, C // 2:C // 2 + 1]
    scores = jnp.einsum('bnihd,bnjhd->bnhij', q * jnp.exp(gcs - ref), k * jnp.exp(ref - gcs))
    causal = jnp.tril(jnp.ones((C, C), dtype=bool))
    scores = jnp.where(causal, scores, 0.0)
    o_intra = jnp.einsum('bnhij,bnjhv->bnihv', scores, v)
    g_last = gcs[:, :, -1]
    chunk_kv = jnp.einsum('bnjhd,bnjhv->bnhdv', k * jnp.exp(g_last[:, :, None] - gcs), v)

    def carry_state(s, inp):
        decay, kv = inp
        return decay[..., None] * s + kv, s

    _, prev_states = lax.scan(carry_state, jnp.zeros_like(chunk_kv[:, 0]), (jnp.moveaxis(jnp.exp(g_last), 1, 0), jnp.moveaxis(chunk_kv, 1, 0)))
    prev_states = jnp.moveaxis(prev_states, 0, 1)
    o_inter = jnp.einsum('bnihd,bnhdv->bnihv', q * jnp.exp(gcs), prev_states)
    return (o_intra + o_inter).reshape(b, L, H, dv)

def ssd_gla_layer(x, norm_w, w_in, conv_w, conv_b, a_log, dt_bias, d_skip, ssd_norm_w, gate_w2, gate_b, gla_norm_w, w_out):
    bsz, L, _ = x.shape
    h = rms_norm(x, norm_w)
    u = h @ w_in.astype(jnp.float32)
    z_a, xbc, dt_raw, q_b, k_b, v_b, gate_lr, g_b = split_cols(u, EVEN_SPLITS)
    xbc = jax.nn.silu(causal_depthwise_conv(xbc, conv_w, conv_b))
    xs, bm, cm = split_cols(xbc, (SSD_WIDTH, SSD_GROUPS * SSD_STATE, SSD_GROUPS * SSD_STATE))
    xs = xs.reshape(bsz, L, SSD_GROUPS, SSD_HEADS_PER_GROUP, SSD_HEAD_DIM)
    bm = bm.reshape(bsz, L, SSD_GROUPS, SSD_STATE)
    cm = cm.reshape(bsz, L, SSD_GROUPS, SSD_STATE)
    dt = jax.nn.softplus(dt_raw + dt_bias.astype(jnp.float32)).reshape(bsz, L, SSD_GROUPS, SSD_HEADS_PER_GROUP)
    a = -jnp.exp(a_log.astype(jnp.float32)).reshape(SSD_GROUPS, SSD_HEADS_PER_GROUP)
    d = d_skip.astype(jnp.float32).reshape(SSD_GROUPS, SSD_HEADS_PER_GROUP)
    y_a = ssd_chunked_scan(xs, dt, a, bm, cm, d)
    y_a = rms_norm(y_a * jax.nn.silu(z_a), ssd_norm_w)
    q_b = q_b.reshape(bsz, L, GLA_HEADS, GLA_HEAD_K) * (GLA_HEAD_K ** -0.5)
    k_b = k_b.reshape(bsz, L, GLA_HEADS, GLA_HEAD_K)
    v_b = v_b.reshape(bsz, L, GLA_HEADS, GLA_HEAD_V)
    log_decay = jax.nn.log_sigmoid(gate_lr @ gate_w2.astype(jnp.float32) + gate_b.astype(jnp.float32)) / GLA_GATE_NORMALIZER
    log_decay = log_decay.reshape(bsz, L, GLA_HEADS, GLA_HEAD_K)
    o_b = gla_chunked(q_b, k_b, v_b, log_decay)
    o_b = rms_norm(o_b, gla_norm_w).reshape(bsz, L, GLA_VALUE_WIDTH) * jax.nn.silu(g_b)
    out = jnp.concatenate([y_a, o_b], axis=-1) @ w_out.astype(jnp.float32)
    return x + out.astype(x.dtype)

def moba_attention(q, k, v):
    b, H, L, d = q.shape
    nb = -(-L // MOBA_BLOCK)
    lp = nb * MOBA_BLOCK
    pad = ((0, 0), (0, 0), (0, lp - L), (0, 0))
    q = jnp.pad(q * (d ** -0.5), pad)
    k = jnp.pad(k, pad)
    v = jnp.pad(v, pad)
    kb = k.reshape(b, H, nb, MOBA_BLOCK, d)
    vb = v.reshape(b, H, nb, MOBA_BLOCK, d)
    k_mean = jnp.mean(kb, axis=3)
    gate = jnp.einsum('bhqd,bhnd->bhqn', q, k_mean).astype(jnp.float32)
    n_past_all = jnp.arange(lp) // MOBA_BLOCK
    fully_past = jnp.arange(nb)[None, :] < n_past_all[:, None]
    gate = jnp.where(fully_past, gate, -jnp.inf)
    k_sel = min(MOBA_TOPK, nb)
    _, top_idx = lax.top_k(gate, k_sel)
    bi = jnp.arange(b)[:, None, None]
    hi = jnp.arange(H)[None, :, None]

    def attend_chunk(start):
        qc = lax.dynamic_slice_in_dim(q, start, MOBA_Q_CHUNK, axis=2)
        idx_c = lax.dynamic_slice_in_dim(top_idx, start, MOBA_Q_CHUNK, axis=2)
        pos = start + jnp.arange(MOBA_Q_CHUNK)
        n_past = pos // MOBA_BLOCK
        logits = []
        for s in range(k_sel):
            ks = kb[bi, hi, idx_c[..., s]]
            ls = jnp.einsum('bhqd,bhqkd->bhqk', qc, ks).astype(jnp.float32)
            logits.append(jnp.where((s < n_past)[:, None], ls, -jnp.inf))
        own = start // MOBA_BLOCK
        ko = lax.dynamic_index_in_dim(kb, own, axis=2, keepdims=False)
        vo = lax.dynamic_index_in_dim(vb, own, axis=2, keepdims=False)
        lo = jnp.einsum('bhqd,bhkd->bhqk', qc, ko).astype(jnp.float32)
        key_pos = own * MOBA_BLOCK + jnp.arange(MOBA_BLOCK)
        logits.append(jnp.where(key_pos[None, :] <= pos[:, None], lo, -jnp.inf))
        p = jax.nn.softmax(jnp.concatenate(logits, axis=-1), axis=-1)
        p_parts = jnp.split(p, k_sel + 1, axis=-1)
        out = jnp.einsum('bhqk,bhkd->bhqd', p_parts[-1].astype(vo.dtype), vo)
        for s in range(k_sel):
            vs = vb[bi, hi, idx_c[..., s]]
            out = out + jnp.einsum('bhqk,bhqkd->bhqd', p_parts[s].astype(vs.dtype), vs)
        return out

    starts = jnp.arange(lp // MOBA_Q_CHUNK) * MOBA_Q_CHUNK
    outs = lax.map(attend_chunk, starts)
    out = jnp.moveaxis(outs, 0, 2).reshape(b, H, lp, d)
    return out[:, :, :L]

def moba_layer(x, norm_w, w_in, w_out):
    bsz, L, _ = x.shape
    h = rms_norm(x, norm_w)
    u = h @ w_in.astype(jnp.float32)
    q, k, v, z = split_cols(u, (MOBA_WIDTH, MOBA_WIDTH, MOBA_WIDTH, MOBA_WIDTH))
    to_heads = lambda t: t.reshape(bsz, L, MOBA_HEADS, MOBA_HEAD_DIM).transpose(0, 2, 1, 3)
    o = moba_attention(to_heads(q), to_heads(k), to_heads(v))
    o = o.transpose(0, 2, 1, 3).reshape(bsz, L, MOBA_WIDTH) * jax.nn.silu(z)
    return x + (o @ w_out.astype(jnp.float32)).astype(x.dtype)

def second_inputs(seed: int = 0) -> dict:
    key = jax.random.key(seed)
    ks = jax.random.split(key, 20)
    nrm = jax.random.normal
    f32 = jnp.float32
    dt_init = jnp.exp(jax.random.uniform(ks[6], (N_EVEN, SSD_HEADS), f32, np.log(1e-3), np.log(1e-1)))
    return {
        'x': nrm(ks[0], (BATCH, SEQ, D_MODEL), f32),
        'even_norm': 1.0 + 0.02 * nrm(ks[1], (N_EVEN, D_MODEL), f32),
        'even_w_in': nrm(ks[2], (N_EVEN, D_MODEL, EVEN_IN_WIDTH), f32) * D_MODEL ** -0.5,
        'even_conv_w': nrm(ks[3], (N_EVEN, SSD_CONV, SSD_CONV_DIM), f32) * SSD_CONV ** -0.5,
        'even_conv_b': 0.02 * nrm(ks[4], (N_EVEN, SSD_CONV_DIM), f32),
        'even_a_log': jnp.log(jax.random.uniform(ks[5], (N_EVEN, SSD_HEADS), f32, 1.0, 16.0)),
        'even_dt_bias': dt_init + jnp.log(-jnp.expm1(-dt_init)),
        'even_d_skip': 1.0 + 0.1 * nrm(ks[7], (N_EVEN, SSD_HEADS), f32),
        'even_ssd_norm': 1.0 + 0.02 * nrm(ks[8], (N_EVEN, SSD_WIDTH), f32),
        'even_gate_w2': nrm(ks[9], (N_EVEN, GLA_GATE_RANK, GLA_KEY_WIDTH), f32) * GLA_GATE_RANK ** -0.5,
        'even_gate_b': 0.1 * nrm(ks[10], (N_EVEN, GLA_KEY_WIDTH), f32),
        'even_gla_norm': 1.0 + 0.02 * nrm(ks[11], (N_EVEN, GLA_HEAD_V), f32),
        'even_w_out': nrm(ks[12], (N_EVEN, EVEN_MIX_WIDTH, D_MODEL), f32) * EVEN_MIX_WIDTH ** -0.5,
        'odd_norm': 1.0 + 0.02 * nrm(ks[13], (N_ODD, D_MODEL), f32),
        'odd_w_in': nrm(ks[14], (N_ODD, D_MODEL, ODD_IN_WIDTH), f32) * D_MODEL ** -0.5,
        'odd_w_out': nrm(ks[15], (N_ODD, MOBA_WIDTH, D_MODEL), f32) * MOBA_WIDTH ** -0.5,
        'final_norm': 1.0 + 0.02 * nrm(ks[16], (D_MODEL,), f32),
    }

def second_block(x, even_norm, even_w_in, even_conv_w, even_conv_b, even_a_log, even_dt_bias, even_d_skip, even_ssd_norm, even_gate_w2, even_gate_b, even_gla_norm, even_w_out, odd_norm, odd_w_in, odd_w_out, final_norm):
    for layer in range(DEPTH):
        i = layer // 2
        if layer % 2 == 0:
            x = ssd_gla_layer(x, even_norm[i], even_w_in[i], even_conv_w[i], even_conv_b[i], even_a_log[i], even_dt_bias[i], even_d_skip[i], even_ssd_norm[i], even_gate_w2[i], even_gate_b[i], even_gla_norm[i], even_w_out[i])
        else:
            x = moba_layer(x, odd_norm[i], odd_w_in[i], odd_w_out[i])
    return rms_norm(x, final_norm).astype(x.dtype)


def setup_inputs(seed=0):
    out = dict(first_inputs(seed))
    for name, value in second_inputs(seed + 1).items():
        if name != "x":
            out[name + "_2"] = value
    return out


def reference(
    x, c, ada_w, ada_b, norm_mix, norm_ffn, w_in, gm_ws, gm_bs, gm_vnorm, out_norm_a,
    out_norm_b, w_out, peer_wq, peer_k1, peer_k2, peer_u, peer_v, final_norm, even_norm_2,
    even_w_in_2, even_conv_w_2, even_conv_b_2, even_a_log_2, even_dt_bias_2, even_d_skip_2,
    even_ssd_norm_2, even_gate_w2_2, even_gate_b_2, even_gla_norm_2, even_w_out_2, odd_norm_2,
    odd_w_in_2, odd_w_out_2, final_norm_2,
):
    x = first_block(
        x, c, ada_w, ada_b, norm_mix, norm_ffn, w_in, gm_ws, gm_bs, gm_vnorm, out_norm_a,
        out_norm_b, w_out, peer_wq, peer_k1, peer_k2, peer_u, peer_v, final_norm,
    )
    return second_block(
        x, even_norm_2, even_w_in_2, even_conv_w_2, even_conv_b_2, even_a_log_2, even_dt_bias_2,
        even_d_skip_2, even_ssd_norm_2, even_gate_w2_2, even_gate_b_2, even_gla_norm_2,
        even_w_out_2, odd_norm_2, odd_w_in_2, odd_w_out_2, final_norm_2,
    )


_drawn_inputs = setup_inputs


def setup_inputs(seed=0):
    import zlib

    import numpy as np

    out = dict(_drawn_inputs(seed))
    spreads = {}
    factors = {'gm_vnorm': 3.579,
     'even_conv_b_2': 4.148,
     'even_ssd_norm_2': 4.938,
     'even_gate_b_2': 3.888,
     'even_gla_norm_2': 7.871,
     'odd_norm_2': 8.0,
     'final_norm_2': 2.736}
    for name, (base, spread) in spreads.items():
        noise = np.random.default_rng([zlib.crc32(name.encode()), seed]).standard_normal(out[name].shape)
        drawn = base * np.exp(spread * noise) if base else spread * noise
        out[name] = jnp.asarray(drawn.astype(out[name].dtype))
    for name, factor in factors.items():
        out[name] = (out[name] * factor).astype(out[name].dtype)
    return out
```

```python
from contextlib import ExitStack, contextmanager

import concourse.bass as bass
from concourse import mybir

F32 = mybir.dt.float32
BF16 = mybir.dt.bfloat16
U32 = mybir.dt.uint32
ALU = mybir.AluOpType
ACT = mybir.ActivationFunctionType
AX_X = mybir.AxisListType.X

P = 128
T = 256
TT = T // P
D = 1024
C = D // P
DEPTH = 2
EPS = 1e-6
GROUP = 512
BANK = 512

HEADS = 8
HD = 64
TOPK = 16
HK = HEADS * TOPK
KEYS = 128
EXPERTS = KEYS * KEYS
NEG = -3.0e38

GSLOTS = 8
VSLOTS = 4
VJ = 2

SSD_HEADS = 16
XBC = 10
CONV = 4
GLA_CHUNK = 64
GLA_NORMALIZER = 16.0
MOBA_HEADS = 16


class Names(dict):

    def __getattr__(self, name):
        return self[name]

    def __setattr__(self, name, value):
        self[name] = value


def chain(eng, sem):
    count = [0]

    def link(ins):
        count[0] += 1
        ins.then_inc(sem, 1)
        eng.wait_ge(sem, count[0])
    return link


def stage_maker(nc, clear):
    @contextmanager
    def stage(name):
        with nc.Block(name) as block:
            yield block
        nc.all_engine_barrier(sems_to_clear=clear)
    return stage



def make_constants(nc, m, stage):
    s = m.sem
    with stage("constants") as block:
        @block.gpsimd
        def _(pool):
            link = chain(pool, s.pool_step)
            nc.gpsimd.memset(m.zeros_bf[:], 0.0)
            nc.gpsimd.memset(m.ident[:], 0.0)
            nc.gpsimd.memset(m.ones[:], 1.0)
            nc.gpsimd.memset(m.neg_ones[:], -1.0)
            nc.gpsimd.memset(m.layer_base[:], 0.0)
            nc.gpsimd.memset(m.keep3[:], 1.0)
            nc.gpsimd.memset(m.cap3[:], 0.0)
            nc.gpsimd.memset(m.upto3[:], 1.0)
            nc.gpsimd.memset(m.after[:], 1.0)
            nc.gpsimd.iota(m.count[:], pattern=[[1, P]], base=0, channel_multiplier=0,
                           allow_small_or_imprecise_dtypes=True)
            link(nc.gpsimd.memset(m.neg_tri[:], -1.0))
            nc.gpsimd.affine_select(out=m.ident[:], in_=m.ident[:], compare_op=ALU.not_equal, fill=1.0,
                                    base=0, pattern=[[-1, P]], channel_multiplier=1)
            nc.gpsimd.affine_select(out=m.neg_tri[:], in_=m.neg_tri[:], compare_op=ALU.is_ge, fill=0.0,
                                    base=0, pattern=[[-1, P]], channel_multiplier=1)
            nc.gpsimd.affine_select(out=m.after[:], in_=m.after[:], compare_op=ALU.is_gt, fill=0.0,
                                    base=0, pattern=[[-1, P]], channel_multiplier=1)
            for b in (0, 2):
                nc.gpsimd.affine_select(out=m.keep3[:, b, :], in_=m.keep3[:, b, :], compare_op=ALU.is_gt, fill=0.0,
                                        base=0, pattern=[[1, P]], channel_multiplier=-1)
                nc.gpsimd.affine_select(out=m.cap3[:, b, :], in_=m.cap3[:, b, :], compare_op=ALU.is_gt, fill=NEG,
                                        base=0, pattern=[[1, P]], channel_multiplier=-1)
                nc.gpsimd.affine_select(out=m.upto3[:, b, :], in_=m.upto3[:, b, :], compare_op=ALU.is_ge, fill=0.0,
                                        base=0, pattern=[[1, P]], channel_multiplier=-1)

        @block.sync
        def _(sp):
            nc.sync.dma_start(m.x_tok[:], m.x_dram.rearrange("o (a p) d -> p (o a) d", p=P)).then_inc(s.loaded, 16)
            sp.wait_ge(s.loaded, 16)


def to_feature_major(nc, m, stage, name, src, dst):
    s = m.sem
    with stage(name) as block:
        @block.tensor
        def _(pe):
            for n in range(TT * C // 4):
                t, q = n // (C // 4), n % (C // 4)
                for k in range(4):
                    c = 4 * q + k
                    last = nc.tensor.transpose(m.ps[n][:, k * P:(k + 1) * P], src[:, t, c * P:(c + 1) * P], m.ident[:])
                last.then_inc(s.pe_done, 1)

        @block.vector
        def _(dve):
            for n in range(TT * C // 4):
                t, q = n // (C // 4), n % (C // 4)
                dve.wait_ge(s.pe_done, n + 1)
                nc.vector.tensor_copy(dst[:, 4 * q:4 * q + 4, t * P:(t + 1) * P],
                                      m.ps[n][:].rearrange("p (c t) -> p c t", c=4))


def to_token_major(nc, m, stage, name, src, dst, store=None):
    s = m.sem
    with stage(name) as block:
        @block.tensor
        def _(pe):
            for n in range(TT * C // 4):
                t, q = n // (C // 4), n % (C // 4)
                for k in range(4):
                    last = nc.tensor.transpose(m.ps[n][:, k * P:(k + 1) * P],
                                               src[:, 4 * q + k, t * P:(t + 1) * P], m.ident[:])
                last.then_inc(s.pe_done, 1)

        @block.vector
        def _(dve):
            for n in range(TT * C // 4):
                t, q = n // (C // 4), n % (C // 4)
                dve.wait_ge(s.pe_done, n + 1)
                nc.vector.tensor_copy(dst[:, t, q * BANK:(q + 1) * BANK], m.ps[n][:]).then_inc(s.dve_done, 1)

        if store is not None:
            @block.sync
            def _(sp):
                for t in range(TT):
                    sp.wait_ge(s.dve_done, (t + 1) * C // 4)
                    nc.sync.dma_start(store[t * P:(t + 1) * P, :], dst[:, t, :]).then_inc(s.stored, 16)
                sp.wait_ge(s.stored, 16 * TT)


def load_vectors(nc, m, stage, name, rows, dst):
    s = m.sem
    total = sum(n for _, n in rows)
    with stage(name) as block:
        @block.sync
        def _(sp):
            at = 0
            for src, n in rows:
                nc.sync.dma_start(m.vec_rows[at:at + n, :], src).then_inc(s.loaded, 16)
                at += n

        @block.tensor
        def _(pe):
            pe.wait_ge(s.loaded, 16 * len(rows))
            nc.tensor.transpose(m.ps[0][:, 0:total], m.vec_rows[0:total, :], m.ident[0:total, 0:total]).then_inc(s.pe_done, 1)

        @block.vector
        def _(dve):
            dve.wait_ge(s.pe_done, 1)
            nc.vector.tensor_copy(dst[:, 0:total], m.ps[0][:, 0:total])



def norm(nc, m, stage, name, src, dst, chunks, gain, shift=None, width=None):
    s = m.sem
    width = width or chunks
    sets = chunks // width
    with stage(name) as block:
        @block.scalar
        def _(act):
            for c in range(0, chunks, 2):
                nc.scalar.activation(m.squares[:, c:c + 2, :], src[:, c:c + 2, :], ACT.Square).then_inc(s.act_done, 1)
            for g in range(sets):
                act.wait_ge(s.mean_ready, g + 1)
                nc.scalar.activation(m.root[:, g, :], m.mean[:, g, :], ACT.Sqrt).then_inc(s.root_ready, 1)
            if shift is not None:
                for c in range(chunks):
                    act.wait_ge(s.scaled, c + 1)
                    nc.scalar.activation(dst[:, c, :], dst[:, c, :], ACT.Identity, bias=shift[:, c:c + 1])

        @block.tensor
        def _(pe):
            for g in range(sets):
                for k in range(width):
                    c = g * width + k
                    pe.wait_ge(s.act_done, c // 2 + 1)
                    last = nc.tensor.matmul(m.ps[g][:, 0:T], m.ones[:], m.squares[:, c, :],
                                            start=(k == 0), stop=(k == width - 1))
                last.then_inc(s.pe_done, 1)

        @block.vector
        def _(dve):
            link = chain(dve, s.dve_step)
            for g in range(sets):
                dve.wait_ge(s.pe_done, g + 1)
                nc.vector.tensor_scalar(m.mean[:, g, :], m.ps[g][:, 0:T], 1.0 / (width * P), EPS,
                                        ALU.mult, ALU.add).then_inc(s.mean_ready, 1)
            for g in range(sets):
                dve.wait_ge(s.root_ready, g + 1)
                link(nc.vector.reciprocal(m.rstd[:, g, :], m.root[:, g, :]))
                for k in range(width):
                    c = g * width + k
                    nc.vector.scalar_tensor_tensor(out=dst[:, c, :], in0=src[:, c, :], scalar=gain[:, c:c + 1],
                                                   in1=m.rstd[:, g, :], op0=ALU.mult, op1=ALU.mult).then_inc(s.scaled, 1)



def project(nc, m, stage, name, act_in, kchunks, loads, ring):
    s = m.sem
    width = 8 * GROUP // kchunks
    slots = len(ring)
    views = [r[:].rearrange("p (k n) -> p k n", k=kchunks) for r in ring]
    units = []
    for n, (w, kind, evac) in enumerate(loads):
        cols = w.shape[1]
        for u, (engine, fn) in enumerate(evac):
            units.append((n, u, cols, kind, engine, fn))
    by_engine = {e: [i for i, x in enumerate(units) if x[4] == e] for e in ("act", "dve")}
    done_by = {"act": s.act_done, "dve": s.dve_done}

    def view(i):
        n, u, cols, kind, _, _ = units[i]
        bank = m.ps[i % 8]
        if kind == "token":
            return bank[:, 0:cols]
        if cols < P:
            return bank[0:cols, 0:T]
        return bank[:].rearrange("p (c t) -> p c t", c=2)

    with stage(name) as block:
        @block.sync
        def _(sp):
            for n, (w, kind, evac) in enumerate(loads):
                if n >= slots:
                    sp.wait_ge(s.pe_done, sum(len(x[2]) for x in loads[:n - slots + 1]))
                cols = w.shape[1]
                nc.sync.dma_start(views[n % slots][:, :, 0:cols],
                                  w.rearrange("(k p) n -> p k n", p=P)).then_inc(s.slot_loaded[n % slots], 16)

        @block.tensor
        def _(pe):
            for i, (n, u, cols, kind, engine, fn) in enumerate(units):
                w = views[n % slots]
                if u == 0:
                    pe.wait_ge(s.slot_loaded[n % slots], 16 * (n // slots + 1))
                if i >= 8:
                    before = units[i - 8][4]
                    pe.wait_ge(done_by[before], by_engine[before].index(i - 8) + 1)
                if kind == "token":
                    for k in range(kchunks):
                        last = nc.tensor.matmul(m.ps[i % 8][:, 0:cols], act_in[:, k, u * P:(u + 1) * P], w[:, k, 0:cols],
                                                start=(k == 0), stop=(k == kchunks - 1))
                elif cols < P:
                    for k in range(kchunks):
                        last = nc.tensor.matmul(m.ps[i % 8][0:cols, 0:T], w[:, k, 0:cols], act_in[:, k, :],
                                                start=(k == 0), stop=(k == kchunks - 1))
                else:
                    for h in range(2):
                        f = (2 * u + h) * P
                        for k in range(kchunks):
                            last = nc.tensor.matmul(m.ps[i % 8][:, h * T:(h + 1) * T], w[:, k, f:f + P], act_in[:, k, :],
                                                    start=(k == 0), stop=(k == kchunks - 1))
                last.then_inc(s.pe_done, 1)

        @block.scalar
        def _(act):
            for i in by_engine["act"]:
                act.wait_ge(s.pe_done, i + 1)
                units[i][5](view(i)).then_inc(s.act_done, 1)

        @block.vector
        def _(dve):
            for i in by_engine["dve"]:
                dve.wait_ge(s.pe_done, i + 1)
                units[i][5](view(i)).then_inc(s.dve_done, 1)


def act_fn(nc, dst, func, scale=1.0):
    return ("act", lambda ps: nc.scalar.activation(dst, ps, func, scale=scale))


def dve_copy(nc, dst):
    return ("dve", lambda ps: nc.vector.tensor_copy(dst, ps))


def residual(nc, m, c, gates):
    def run(ps):
        for k in range(2):
            if gates is None:
                last = nc.vector.tensor_tensor(m.x_fm[:, c + k, :], ps[:, k, :], m.x_fm[:, c + k, :], ALU.add)
            else:
                last = nc.vector.scalar_tensor_tensor(out=m.x_fm[:, c + k, :], in0=ps[:, k, :], scalar=gates[:, c + k:c + k + 1],
                                                      in1=m.x_fm[:, c + k, :], op0=ALU.mult, op1=ALU.add)
        return last
    return ("dve", run)



def modulation(nc, m, stage, ada_w, c_rows, ring):
    s = m.sem
    views = [r[:].rearrange("p (k n) -> p k n", k=C) for r in ring]
    slots = len(ring)
    loads = ada_w.shape[1] // GROUP
    per = GROUP // P
    with stage("modulation") as block:
        @block.sync
        def _(sp):
            nc.sync.dma_start(m.c_rows[:], c_rows).then_inc(s.loaded, 16)
            for n in range(loads):
                if n >= slots:
                    sp.wait_ge(s.pe_done, n - slots + 1)
                nc.sync.dma_start(views[n % slots], ada_w[:, n * GROUP:(n + 1) * GROUP].rearrange("(k p) n -> p k n", p=P)
                                  ).then_inc(s.slot_loaded[n % slots], 16)

        @block.tensor
        def _(pe):
            pe.wait_ge(s.loaded, 16)
            nc.tensor.transpose(m.ps[1][:, 0:C], m.c_rows[:], m.ident[0:C, 0:C]).then_inc(s.first, 1)
            pe.wait_ge(s.act_done, 1)
            for n in range(loads):
                pe.wait_ge(s.slot_loaded[n % slots], 16 * (n // slots + 1))
                for f in range(per):
                    for k in range(C):
                        last = nc.tensor.matmul(m.ps[0][:, n * per + f:n * per + f + 1], views[n % slots][:, k, f * P:(f + 1) * P],
                                                m.c_act[:, k:k + 1], start=(k == 0), stop=(k == C - 1))
                last.then_inc(s.pe_done, 1)

        @block.scalar
        def _(act):
            act.wait_ge(s.first, 1)
            nc.scalar.activation(m.c_act[:], m.ps[1][:, 0:C], ACT.Silu).then_inc(s.act_done, 1)

        @block.vector
        def _(dve):
            link = chain(dve, s.dve_step)
            dve.wait_ge(s.pe_done, loads)
            link(nc.vector.tensor_tensor(m.mod[:], m.ps[0][:, 0:6 * C], m.vecs[:, 0:6 * C], ALU.add))
            for g, sc, nv in ((0, 1, 6 * C), (1, 4, 7 * C)):
                nc.vector.scalar_tensor_tensor(out=m.gain[:, g * C:(g + 1) * C], in0=m.mod[:, sc * C:(sc + 1) * C], scalar=1.0,
                                               in1=m.vecs[:, nv:nv + C], op0=ALU.add, op1=ALU.mult)



def gmlp(nc, m, stage, ws, bs, vnorm):
    s = m.sem
    a = m.a
    with stage("gmlp") as block:
        @block.sync
        def _(sp):
            nc.sync.dma_start(a.gain_row[:], vnorm.to_broadcast([P, HEADS * HD])).then_inc(s.loaded, 16)
            nc.sync.dma_start(a.ws[:], ws.rearrange("h t s -> t h s")).then_inc(s.slot_loaded[0], 16)
            nc.sync.dma_start(a.bias_row[:], bs.rearrange("(o h) t -> o (h t)", o=1)).then_inc(s.slot_loaded[1], 16)

        @block.scalar
        def _(act):
            nc.scalar.activation(a.v_sq[:], a.v_gelu[:], ACT.Square).then_inc(s.first, 1)
            act.wait_ge(s.mean_ready, 1)
            nc.scalar.activation(a.v_root[:], a.v_mean[:], ACT.Sqrt).then_inc(s.root_ready, 1)
            for n in range(2):
                act.wait_ge(s.pe_done, n + 1)
                nc.scalar.activation(a.ws_t[:, 4 * n:4 * n + 4, :], m.ps[n][:].rearrange("p (h t) -> p h t", h=4),
                                     ACT.Copy).then_inc(s.act_done, 1)

        @block.gpsimd
        def _(pool):
            pool.wait_ge(s.act_done, 2)
            nc.gpsimd.memset(a.ws_t[HD:P, :, 0:HD], 0.0).then_inc(s.masked, 1)

        @block.tensor
        def _(pe):
            pe.wait_ge(s.slot_loaded[0], 16)
            for n in range(2):
                for k in range(4):
                    last = nc.tensor.transpose(m.ps[n][:, k * P:(k + 1) * P], a.ws[:, 4 * n + k, :], m.ident[:])
                last.then_inc(s.pe_done, 1)
            pe.wait_ge(s.slot_loaded[1], 16)
            pe.wait_ge(s.masked, 1)
            pe.wait_ge(s.normed, 1)
            for h in range(HEADS):
                lo = HD * (h % 2)
                bank = m.ps[2 + h // 2]
                for n in range(TT):
                    out = bank[lo:lo + HD, n * P:(n + 1) * P]
                    nc.tensor.matmul(out, a.v_norm[:, n, h * HD:(h + 1) * HD], a.ws_t[:, h, :], start=True, stop=False)
                    last = nc.tensor.matmul(out, m.ones[0:1, 0:HD], a.bias_row[0:1, h * P:(h + 1) * P], start=False, stop=True)
                last.then_inc(s.pe_done, 1)

        @block.vector
        def _(dve):
            link = chain(dve, s.dve_step)
            dve.wait_ge(s.first, 1)
            link(nc.vector.tensor_reduce(a.v_mean[:], a.v_sq[:].rearrange("p n (h c) -> p (n h) c", c=HD), AX_X, ALU.add))
            nc.vector.tensor_scalar(a.v_mean[:], a.v_mean[:], 1.0 / HD, EPS, ALU.mult, ALU.add).then_inc(s.mean_ready, 1)
            dve.wait_ge(s.root_ready, 1)
            link(nc.vector.reciprocal(a.v_rstd[:], a.v_root[:]))
            link(nc.vector.tensor_tensor(a.v_norm[:].rearrange("p n (h c) -> p (n h) c", c=HD),
                                         a.v_gelu[:].rearrange("p n (h c) -> p (n h) c", c=HD),
                                         a.v_rstd[:].rearrange("p (h o) -> p h o", o=1).to_broadcast([P, TT * HEADS, HD]), ALU.mult))
            dve.wait_ge(s.loaded, 16)
            nc.vector.tensor_tensor(a.v_norm[:], a.v_norm[:],
                                    a.gain_row[:].rearrange("p (o n) -> p o n", o=1).to_broadcast([P, TT, HEADS * HD]),
                                    ALU.mult).then_inc(s.normed, 1)
            for c in range(HEADS // 2):
                dve.wait_ge(s.pe_done, 2 + 2 * (c + 1))
                nc.vector.tensor_tensor(a.y[:, c, :], m.ps[2 + c][:, 0:T], a.u_gelu[:, c, :], ALU.mult)



def stick_breaking(nc, m, stage):
    s = m.sem
    a = m.a
    W3 = 3 * P
    cols = lambda x: x.rearrange("p (b t) -> p b t", b=3)
    with stage("stick") as block:
        @block.tensor
        def _(pe):
            def scores(h):
                lo, c = HD * (h % 2), h // 2
                k, q = a.k_fm[lo:lo + HD, c, :], a.q_fm[lo:lo + HD, c, :]
                if h >= 4:
                    pe.wait_ge(s.capped, h - 3)
                z = m.ps[h % 4]
                nc.tensor.matmul(z[:, 0:T], k[:, 0:P], q, start=True, stop=False, skip_group_check=True)
                nc.tensor.matmul(z[:, T:W3], k[:, P:T], q[:, P:T], start=False, stop=False,
                                 skip_group_check=True).then_inc(s.scores_ready, 1)

            def sums(h):
                pe.wait_ge(s.sp_ready, h + 1)
                z, sp = m.ps[h % 4], a.sp[:, h % 2, :]
                nc.tensor.matmul(z[:, 0:W3], m.neg_tri[:], sp, start=False, stop=False, skip_group_check=True)
                nc.tensor.matmul(z[:, P:T], m.neg_ones[:], sp[:, T:W3], start=False, stop=True,
                                 skip_group_check=True).then_inc(s.logs_ready, 1)

            def values(h):
                pe.wait_ge(s.probs_ready, h + 1)
                lo = HD * (h % 2)
                out, pr = m.ps[4 + h // 2][lo:lo + HD, :], a.probs[:, h % 2, :]
                nc.tensor.matmul(out[:, 0:T], a.v_tok[:, 0, h * HD:(h + 1) * HD], pr[:, 0:T], start=True, stop=False,
                                 skip_group_check=True)
                nc.tensor.matmul(out[:, P:T], a.v_tok[:, 1, h * HD:(h + 1) * HD], pr[:, T:W3], start=False, stop=True,
                                 skip_group_check=True).then_inc(s.values_ready, 1)

            for i in range(HEADS + 2):
                if i < HEADS:
                    scores(i)
                if 1 <= i < HEADS + 1:
                    sums(i - 1)
                if i >= 2:
                    values(i - 2)

        @block.vector
        def _(dve):
            link = chain(dve, s.dve_step)

            def softplus(h):
                dve.wait_ge(s.log_ready, h + 1)
                if h >= 2:
                    dve.wait_ge(s.logs_ready, h - 1)
                link(nc.vector.scalar_tensor_tensor(out=a.sp[:, h % 2, :], in0=m.ps[h % 4][:, 0:W3], scalar=0.0,
                                                    in1=a.lnp[:, h % 2, :], op0=ALU.max, op1=ALU.add))
                nc.vector.tensor_tensor(cols(a.sp[:, h % 2, :]), cols(a.sp[:, h % 2, :]), m.keep3[:], ALU.mult
                                        ).then_inc(s.sp_ready, 1)

            def cap(h):
                dve.wait_ge(s.logs_ready, h + 1)
                if h >= 2:
                    dve.wait_ge(s.probs_ready, h - 1)
                nc.vector.tensor_tensor(cols(a.loga[:, h % 2, :]), cols(m.ps[h % 4][:, 0:W3]), m.cap3[:], ALU.min
                                        ).then_inc(s.capped, 1)

            def out(h):
                if h % 2:
                    dve.wait_ge(s.values_ready, h + 1)
                    nc.vector.tensor_copy(a.y[:, 4 + h // 2, :], m.ps[4 + h // 2][:, 0:T])

            for i in range(HEADS + 2):
                if 1 <= i < HEADS + 1:
                    softplus(i - 1)
                if 1 <= i < HEADS + 1:
                    cap(i - 1)
                if i >= 2:
                    out(i - 2)

        @block.scalar
        def _(act):
            for i in range(HEADS + 1):
                if i < HEADS:
                    h = i
                    act.wait_ge(s.scores_ready, h + 1)
                    if h >= 2:
                        act.wait_ge(s.exp_done, h - 1)
                    nc.scalar.activation(a.absz[:, h % 2, :], m.ps[h % 4][:, 0:W3], ACT.Abs).then_inc(s.abs_ready, 1)
                    act.wait_ge(s.abs_ready, h + 1)
                    if h >= 2:
                        act.wait_ge(s.log_ready, h - 1)
                    nc.scalar.activation(a.expz[:, h % 2, :], a.absz[:, h % 2, :], ACT.Exp, scale=-1.0).then_inc(s.exp_done, 1)
                    act.wait_ge(s.exp_done, h + 1)
                    if h >= 2:
                        act.wait_ge(s.sp_ready, h - 1)
                    nc.scalar.activation(a.lnp[:, h % 2, :], a.expz[:, h % 2, :], ACT.Ln, bias=1.0).then_inc(s.log_ready, 1)
                if i >= 1:
                    h = i - 1
                    act.wait_ge(s.capped, h + 1)
                    if h >= 2:
                        act.wait_ge(s.values_ready, h - 1)
                    nc.scalar.activation(a.probs[:, h % 2, :], a.loga[:, h % 2, :], ACT.Exp).then_inc(s.probs_ready, 1)



def router(nc, m, stage, k1, k2):
    s = m.sem
    a = m.a
    SEG = TT * HEADS * 2
    PAIR = TT * HEADS
    with stage("router") as block:
        @block.sync
        def _(sp):
            nc.sync.dma_start(a.key_table[:, 0, :], k1).then_inc(s.loaded, 16)
            nc.sync.dma_start(a.key_table[:, 1, :], k2).then_inc(s.loaded, 16)

        @block.tensor
        def _(pe):
            pe.wait_ge(s.loaded, 32)
            for x in range(2):
                last = nc.tensor.transpose(m.ps[7][:, x * P:(x + 1) * P], a.key_table[:, x, :], m.ident[:])
            last.then_inc(s.first, 1)
            pe.wait_ge(s.act_done, 1)
            for n in range(8):
                t, hp = n // 4, n % 4
                if n == 7:
                    pe.wait_ge(s.act_done, 2)
                for x in range(4):
                    half = x % 2
                    last = nc.tensor.matmul(m.ps[n][:, x * KEYS:(x + 1) * KEYS], a.query[:, 4 * hp + x, t * P:(t + 1) * P],
                                            a.keys_t[:, half, :], start=True, stop=True)
                last.then_inc(s.pe_done, 1)

            pe.wait_ge(s.normed, 1)
            for x in range(2):
                for t in range(TT):
                    last = nc.tensor.transpose(m.ps[x][:, t * P:(t + 1) * P], a.chosen[:, x, t, :], m.ident[:])
                last.then_inc(s.values_ready, 1)

        @block.scalar
        def _(act):
            act.wait_ge(s.first, 1)
            nc.scalar.activation(a.keys_t[:], m.ps[7][:, 0:2 * P].rearrange("p (x k) -> p x k", x=2), ACT.Copy).then_inc(s.act_done, 1)
            for n in range(8):
                act.wait_ge(s.pe_done, n + 1)
                nc.scalar.activation(a.scores[:, 4 * n:4 * n + 4, :], m.ps[n][:].rearrange("p (x k) -> p x k", x=4),
                                     ACT.Copy).then_inc(s.act_done, 1)
            act.wait_ge(s.abs_ready, 1)
            nc.scalar.activation(a.gate[:], a.gate[:], ACT.Exp).then_inc(s.exp_done, 1)
            for x, dst in ((0, m.key1_t), (1, m.key2_t)):
                act.wait_ge(s.values_ready, x + 1)
                nc.scalar.activation(dst[:], m.ps[x][:, 0:T], ACT.Copy)

        @block.vector
        def _(dve):
            link = chain(dve, s.dve_step)

            def top16(values, spare, best, where, segments, waits):
                for g in range(segments):
                    if waits and g % 4 == 0:
                        dve.wait_ge(s.act_done, 2 + g // 4)
                    last = nc.vector.max(out=best[:, g, 0:8], in_=values[:, g, :])
                link(last)
                for g in range(segments):
                    nc.vector.max_index(out=where[:, g, 0:8], in_max=best[:, g, 0:8], in_values=values[:, g, :])
                    last = nc.vector.match_replace(out=spare[:, g, :], in_to_replace=best[:, g, 0:8], in_values=values[:, g, :],
                                                   imm_value=NEG)
                link(last)
                for g in range(segments):
                    last = nc.vector.max(out=best[:, g, 8:16], in_=spare[:, g, :])
                link(last)
                for g in range(segments):
                    last = nc.vector.max_index(out=where[:, g, 8:16], in_max=best[:, g, 8:16], in_values=spare[:, g, :])
                link(last)

            top16(a.scores, a.spare, a.best, a.where, SEG, True)
            nc.vector.tensor_copy(a.key_no[:], a.where[:])
            halves = a.best[:].rearrange("p (g x) k -> p g x k", x=2)
            for t in range(TT):
                g = slice(t * HEADS, (t + 1) * HEADS)
                first = halves[:, g, 0, :].rearrange("p g (i o) -> p g i o", o=1).to_broadcast([P, HEADS, TOPK, TOPK])
                second = halves[:, g, 1, :].rearrange("p g (o j) -> p g o j", o=1).to_broadcast([P, HEADS, TOPK, TOPK])
                last = nc.vector.tensor_tensor(a.pairs[:, g, :].rearrange("p g (i j) -> p g i j", i=TOPK), first, second, ALU.add)
            link(last)
            top16(a.pairs, a.pair_spare, a.top, a.place, PAIR, False)
            nc.vector.tensor_tensor(a.gate[:], a.top[:], a.top[:, :, 0:1].to_broadcast([P, PAIR, TOPK]),
                                    ALU.subtract).then_inc(s.abs_ready, 1)
            nc.vector.tensor_scalar(a.place_ij[:, 0, :, :], a.place[:], 4, None, ALU.logical_shift_right)
            link(nc.vector.tensor_scalar(a.place_ij[:, 1, :, :], a.place[:], 15, None, ALU.bitwise_and))
            link(nc.vector.tensor_copy(a.place_no[:], a.place_ij[:]))
            numbers = a.key_no[:].rearrange("p (g x) k -> p g x k", x=2)
            slots = m.count[:, 0:TOPK].rearrange("p (o k) -> p o k", o=1).to_broadcast([P, HK, TOPK])
            for t in range(TT):
                g = slice(t * HEADS, (t + 1) * HEADS)
                for x in range(2):
                    at = a.place_no[:, x, g, :].rearrange("p g (k o) -> p (g k) o", o=1).to_broadcast([P, HK, TOPK])
                    link(nc.vector.tensor_tensor(a.hits[:], at, slots, ALU.is_equal))
                    own = numbers[:, g, x, :].rearrange("p g (o i) -> p g o i", o=1).to_broadcast([P, HEADS, TOPK, TOPK])
                    hits4 = a.hits[:].rearrange("p (g k) i -> p g k i", g=HEADS)
                    link(nc.vector.tensor_tensor(hits4, hits4, own, ALU.mult))
                    link(nc.vector.tensor_reduce(a.chosen[:, x, t, :], a.hits[:], AX_X, ALU.add))
            nc.vector.engine_nop().then_inc(s.normed, 1)
            link(nc.vector.scalar_tensor_tensor(out=a.number[:], in0=a.chosen[:, 0, :, :], scalar=float(KEYS),
                                                in1=a.chosen[:, 1, :, :], op0=ALU.mult, op1=ALU.add))
            nc.vector.tensor_scalar(m.expert[:], a.number[:], m.layer_base[:, 0:1], None, ALU.add)
            dve.wait_ge(s.exp_done, 1)
            link(nc.vector.tensor_reduce(a.gate_sum[:], a.gate[:], AX_X, ALU.add))
            link(nc.vector.reciprocal(a.gate_rec[:], a.gate_sum[:]))
            nc.vector.tensor_tensor(m.gate[:].rearrange("p t (h k) -> p (t h) k", k=TOPK), a.gate[:],
                                    a.gate_rec[:].rearrange("p (g o) -> p g o", o=1).to_broadcast([P, PAIR, TOPK]), ALU.mult)
            link(nc.vector.tensor_scalar(m.layer_base[:], m.layer_base[:], float(EXPERTS), None, ALU.add))


def experts(nc, m, stage, u_table, layer):
    s = m.sem
    SUB = TOPK // GSLOTS
    QUAD = BANK // P
    QUADS = P // QUAD
    PER = TOPK // QUAD
    HOT = 2
    with stage("experts") as block:
        @block.gpsimd
        def _(pool):
            pool.sem_inc(s.slot_free, GSLOTS)
            for t in range(TT):
                with pool.Fori(0, HEADS) as h:
                    for u in range(SUB):
                        base = (t * HEADS + h) * TOPK + u * GSLOTS
                        pool.wait_ge(s.slot_free, base + 1)
                        nc.gpsimd.tensor_copy(m.index[u][:], m.expert[:, t, bass.ds(h * TOPK + u * GSLOTS, GSLOTS)]
                                              ).then_inc(s.index_ready, 1)
                        pool.wait_ge(s.index_ready, (t * HEADS + h) * SUB + u + 1)
                        for g in range(GSLOTS):
                            pool.wait_ge(s.slot_free, base + g + 1)
                            pool.sem_inc(s.gathers_started, 1)
                            nc.gpsimd.indirect_dma_start(
                                out=m.rows[g][:], out_offset=None, in_=u_table,
                                in_offset=bass.IndirectOffsetOnAxis(ap=m.index[u][:, g:g + 1], axis=0),
                            ).then_inc(s.rows_loaded[g], 16)

        def onehots(q, slot):
            for k in range(QUAD):
                tok = q * QUAD + k
                nc.vector.tensor_scalar(m.hot1[:, slot, k, :], m.count[:], m.key1_t[:, bass.ds(tok, 1)],
                                        m.weight_t[:, bass.ds(tok, 1)], ALU.is_equal, ALU.mult)
                last = nc.vector.tensor_scalar(m.hot2[:, slot, k, :], m.count[:], m.key2_t[:, bass.ds(tok, 1)], None, ALU.is_equal)
            return last

        @block.vector
        def _(dve):
            def dots(t, h):
                for u in range(SUB):
                    for g in range(GSLOTS):
                        dve.wait_ge(s.rows_loaded[g], 16 * (((layer * TT + t) * HEADS + h) * SUB + u + 1))
                        nc.vector.scalar_tensor_tensor(out=m.rows[g][:], in0=m.rows[g][:], scalar=1.0, in1=m.h_tok[:, t, :],
                                                       op0=ALU.mult, op1=ALU.mult,
                                                       accum_out=m.dots[:, t, bass.ds(h * TOPK + u * GSLOTS + g, 1)]
                                                       ).then_inc(s.slot_free, 1)

            def weights(t):
                dve.wait_ge(s.act_done, t + 1)
                nc.vector.tensor_tensor(m.dots[:, t, :], m.dots[:, t, :], m.gate[:, t, :], ALU.mult).then_inc(s.weighted, 1)
                dve.wait_ge(s.turned, t + 1)
                nc.vector.tensor_copy(m.weight_t[:, t * P:(t + 1) * P], m.ps[7][:, t * P:(t + 1) * P]).then_inc(s.dve_step, 1)
                dve.wait_ge(s.dve_step, t + 1)

            dve.sem_inc(s.quads_placed, HOT)
            with dve.Fori(0, HEADS) as h:
                dots(0, h)
            weights(0)
            with dve.Fori(0, HEADS) as h:
                for r in range(PER):
                    q = h * PER + r
                    dve.wait_ge(s.quads_placed, q + 1)
                    onehots(q, r % HOT).then_inc(s.hot_ready, 1)
                dots(1, h)
            weights(1)
            with dve.Fori(0, QUADS // PER) as h:
                for r in range(PER):
                    q = QUADS + h * PER + r
                    dve.wait_ge(s.quads_placed, q + 1)
                    onehots(q, r % HOT).then_inc(s.hot_ready, 1)

        @block.scalar
        def _(act):
            def gelu(t):
                act.wait_ge(s.slot_free, GSLOTS + (t + 1) * HK)
                nc.scalar.activation(m.dots[:, t, :], m.dots[:, t, :], ACT.Gelu_apprx_tanh).then_inc(s.act_done, 1)

            def spread(t):
                with act.Fori(0, QUADS // PER) as h:
                    for r in range(PER):
                        q = t * QUADS + h * PER + r
                        act.wait_ge(s.quads_placed, HOT + q + 1)
                        nc.scalar.activation(m.weights[:, :, bass.ds(q * QUAD, QUAD)],
                                             m.ps[r][:].rearrange("p (t j) -> p j t", t=QUAD), ACT.Copy).then_inc(s.spread, 1)

            gelu(0)
            spread(0)
            gelu(1)
            spread(1)

        @block.tensor
        def _(pe):
            pe.sem_inc(s.spread, PER)

            def turn(t):
                pe.wait_ge(s.weighted, t + 1)
                nc.tensor.transpose(m.ps[7][:, t * P:(t + 1) * P], m.dots[:, t, :], m.ident[:]).then_inc(s.turned, 1)

            def place(t):
                with pe.Fori(0, QUADS // PER) as h:
                    for r in range(PER):
                        q = t * QUADS + h * PER + r
                        pe.wait_ge(s.hot_ready, q + 1)
                        pe.wait_ge(s.spread, q + 1)
                        for k in range(QUAD):
                            last = nc.tensor.matmul(m.ps[r][:, k * KEYS:(k + 1) * KEYS], m.hot1[:, r % HOT, k, :],
                                                    m.hot2[:, r % HOT, k, :], start=True, stop=True)
                        last.then_inc(s.quads_placed, 1)

            turn(0)
            place(0)
            turn(1)
            place(1)


def expert_values(nc, m, stage, v_table, gates, ring):
    s = m.sem
    v = v_table.rearrange("(i j) d -> i j d", i=KEYS)
    views = [r[:].rearrange("p (j d) -> p j d", j=VJ) for r in ring]
    steps = KEYS // (VJ * VSLOTS)
    with stage("values") as block:
        @block.sync
        def _(sp):
            sp.sem_inc(s.slot_free, VSLOTS)
            with sp.Fori(0, steps) as i:
                for n in range(VSLOTS):
                    sp.wait_ge(s.slot_free, i * VSLOTS + n + 1)
                    nc.sync.dma_start(views[n], v[:, bass.ds((i * VSLOTS + n) * VJ, VJ), :]).then_inc(s.slot_loaded[n], 16)

        @block.tensor
        def _(pe):
            for b in range(4):
                nc.tensor.matmul(m.ps[b][:], m.zeros_bf[:, 0:P], m.zeros_bf[:], start=True, stop=False, skip_group_check=True)
            with pe.Fori(0, steps) as i:
                for n in range(VSLOTS):
                    pe.wait_ge(s.slot_loaded[n], 16 * (i + 1))
                    for j in range(VJ):
                        for c in range(C):
                            last = nc.tensor.matmul(m.ps[c // 2][:, (c % 2) * T:(c % 2 + 1) * T], views[n][:, j, c * P:(c + 1) * P],
                                                    m.weights[:, bass.ds((i * VSLOTS + n) * VJ + j, 1), :].rearrange("p o t -> p (o t)"),
                                                    start=False, stop=False, skip_group_check=True)
                    last.then_inc(s.slot_free, 1)

        @block.vector
        def _(dve):
            dve.wait_ge(s.slot_free, VSLOTS + KEYS // VJ)
            for c in range(C):
                nc.vector.scalar_tensor_tensor(out=m.x_fm[:, c, :], in0=m.ps[c // 2][:, (c % 2) * T:(c % 2 + 1) * T],
                                               scalar=gates[:, c:c + 1], in1=m.x_fm[:, c, :], op0=ALU.mult, op1=ALU.add)



def convolve(nc, m, stage):
    s = m.sem
    a = m.a
    with stage("convolve") as block:
        @block.vector
        def _(dve):
            link = chain(dve, s.dve_step)
            link(nc.vector.memset(a.xbc[:, :, 0:CONV - 1], 0.0))
            for k in range(CONV):
                for c in range(XBC):
                    tap = m.vecs[:, m.v_conv + k * XBC + c:m.v_conv + k * XBC + c + 1]
                    x = a.xbc[:, c, k:k + T]
                    if k == 0:
                        last = nc.vector.tensor_scalar(a.conv[:, c, :], x, tap, None, ALU.mult)
                    else:
                        last = nc.vector.scalar_tensor_tensor(out=a.conv[:, c, :], in0=x, scalar=tap, in1=a.conv[:, c, :],
                                                              op0=ALU.mult, op1=ALU.add)
                    if k == CONV - 1:
                        last.then_inc(s.dve_done, 1)
                if k < CONV - 1:
                    link(last)

        @block.scalar
        def _(act):
            for c in range(XBC):
                act.wait_ge(s.dve_done, c + 1)
                nc.scalar.activation(a.conv[:, c, :], a.conv[:, c, :], ACT.Silu,
                                     bias=m.vecs[:, m.v_conv_b + c:m.v_conv_b + c + 1])


def ssd(nc, m, stage, a_log, dt_bias, d_skip):
    s = m.sem
    a = m.a
    W3 = 3 * P
    with stage("ssd_prepare") as block:
        @block.sync
        def _(sp):
            row = lambda x: x.to_broadcast([P, SSD_HEADS])
            nc.sync.dma_start(a.a_row[:], row(a_log)).then_inc(s.loaded, 16)
            nc.sync.dma_start(a.dt_row[:], row(dt_bias)).then_inc(s.loaded, 16)
            for x in range(2):
                nc.sync.dma_start(a.d_col[HD * x:HD * (x + 1), :],
                                  d_skip.rearrange("o (c x) -> o c x", x=2)[:, :, x].to_broadcast([HD, C]),
                                  allow_slow_non_contiguous=True).then_inc(s.loaded, 16)
            sp.wait_ge(s.loaded, 64)

        @block.tensor
        def _(pe):
            for n in range(4):
                t, q = n // 2, n % 2
                for k in range(4):
                    last = nc.tensor.transpose(m.ps[n][:, k * P:(k + 1) * P], a.conv[:, 4 * q + k, t * P:(t + 1) * P], m.ident[:])
                last.then_inc(s.pe_done, 1)
            for g in range(2):
                b, c = a.conv[HD * g:HD * (g + 1), 8, :], a.conv[HD * g:HD * (g + 1), 9, :]
                nc.tensor.matmul(m.ps[4 + g][:, 0:T], b[:, 0:P], c, start=True, stop=False, skip_group_check=True)
                nc.tensor.matmul(m.ps[4 + g][:, T:W3], b[:, P:T], c[:, P:T], start=False, stop=True,
                                 skip_group_check=True).then_inc(s.pe_done, 1)

        @block.vector
        def _(dve):
            link = chain(dve, s.dve_step)
            dve.wait_ge(s.loaded, 64)
            link(nc.vector.tensor_tensor(a.dt[:], a.dt_raw[:], a.dt_row[:].rearrange("p (o h) -> p o h", o=1
                                                                                 ).to_broadcast([P, TT, SSD_HEADS]), ALU.add))
            nc.vector.scalar_tensor_tensor(out=a.dt_abs[:], in0=a.dt[:], scalar=-1.0, in1=a.dt[:], op0=ALU.mult, op1=ALU.max).then_inc(s.abs_ready, 1)
            for n in range(4):
                t, q = n // 2, n % 2
                dve.wait_ge(s.pe_done, n + 1)
                nc.vector.tensor_copy(a.xs_tok[:, t, q * BANK:(q + 1) * BANK], m.ps[n][:])
            for g in range(2):
                dve.wait_ge(s.pe_done, 5 + g)
                nc.vector.tensor_tensor(a.cb[:, g, :].rearrange("p (b i) -> p b i", b=3),
                                        m.ps[4 + g][:, 0:W3].rearrange("p (b i) -> p b i", b=3), m.upto3[:], ALU.mult)
            dve.wait_ge(s.act_done, 3)
            link(nc.vector.scalar_tensor_tensor(out=a.dt[:], in0=a.dt[:], scalar=0.0, in1=a.dt_ln[:], op0=ALU.max, op1=ALU.add))
            nc.vector.scalar_tensor_tensor(out=a.dta[:], in0=a.dt[:], scalar=-1.0,
                                           in1=a.a_exp[:].rearrange("p (o h) -> p o h", o=1).to_broadcast([P, TT, SSD_HEADS]),
                                           op0=ALU.mult, op1=ALU.mult)

        @block.scalar
        def _(act):
            act.wait_ge(s.loaded, 64)
            nc.scalar.activation(a.a_exp[:], a.a_row[:], ACT.Exp).then_inc(s.act_done, 1)
            act.wait_ge(s.abs_ready, 1)
            nc.scalar.activation(a.dt_exp[:], a.dt_abs[:], ACT.Exp, scale=-1.0).then_inc(s.act_done, 1)
            act.wait_ge(s.act_done, 2)
            nc.scalar.activation(a.dt_ln[:], a.dt_exp[:], ACT.Ln, bias=1.0).then_inc(s.act_done, 1)

    with stage("ssd") as block:
        @block.vector
        def _(dve):
            def steps(h):
                if h >= 2:
                    dve.wait_ge(s.scores_ready, h - 1)
                b = h % 2
                nc.vector.tensor_scalar(a.steps[:, b, 0, :], m.after[:], a.dta[:, 0, h:h + 1], None, ALU.mult)
                nc.vector.tensor_scalar(a.steps[:, b, 1, :], m.after[:], a.dta[:, 1, h:h + 1], None, ALU.mult)
                nc.vector.tensor_scalar(a.steps[:, b, 2, :], m.ones[:], a.dta[:, 1, h:h + 1], None, ALU.mult
                                        ).then_inc(s.sp_ready, 1)

            def mix(h):
                dve.wait_ge(s.exp_done, h + 1)
                if h >= 2:
                    dve.wait_ge(s.values_ready, h - 1)
                g = h // (SSD_HEADS // 2)
                nc.vector.scalar_tensor_tensor(out=a.mix[:, h % 2, 0:T], in0=a.decay[:, h % 2, 0:T], scalar=a.dt[:, 0, h:h + 1],
                                               in1=a.cb[:, g, 0:T], op0=ALU.mult, op1=ALU.mult)
                nc.vector.scalar_tensor_tensor(out=a.mix[:, h % 2, T:W3], in0=a.decay[:, h % 2, T:W3], scalar=a.dt[:, 1, h:h + 1],
                                               in1=a.cb[:, g, T:W3], op0=ALU.mult, op1=ALU.mult).then_inc(s.probs_ready, 1)

            def out(c):
                dve.wait_ge(s.values_ready, 2 * c + 2)
                nc.vector.scalar_tensor_tensor(out=a.ya[:, c, :], in0=a.conv[:, c, :], scalar=a.d_col[:, c:c + 1],
                                               in1=m.ps[4 + c % 4][:, 0:T], op0=ALU.mult, op1=ALU.add).then_inc(s.dve_done, 1)
                dve.wait_ge(s.dve_done, c + 1)
                nc.vector.tensor_tensor(a.ya[:, c, :], a.ya[:, c, :], a.z_silu[:, c, :], ALU.mult)

            for i in range(SSD_HEADS + 3):
                if i < SSD_HEADS:
                    steps(i)
                if 1 <= i < SSD_HEADS + 1:
                    mix(i - 1)
                if i >= 3 and (i - 3) % 2:
                    out((i - 3) // 2)

        @block.tensor
        def _(pe):
            def sums(h):
                pe.wait_ge(s.sp_ready, h + 1)
                if h >= 4:
                    pe.wait_ge(s.exp_done, h - 3)
                b, seg = h % 2, m.ps[h % 4]
                upto = m.upto3[:].rearrange("p b i -> p (b i)")
                nc.tensor.matmul(seg[:, 0:T], a.steps[:, b, 0, :], upto[:, 0:T], start=True, stop=False, skip_group_check=True)
                nc.tensor.matmul(seg[:, P:T], a.steps[:, b, 2, :], upto[:, 0:P], start=False, stop=False, skip_group_check=True)
                nc.tensor.matmul(seg[:, T:W3], a.steps[:, b, 1, :], upto[:, 0:P], start=False, stop=True,
                                 skip_group_check=True).then_inc(s.scores_ready, 1)

            def products(h):
                pe.wait_ge(s.probs_ready, h + 1)
                if h >= 8:
                    pe.wait_ge(s.dve_done, h // 2 - 3)
                lo = HD * (h % 2)
                out = m.ps[4 + (h // 2) % 4][lo:lo + HD, :]
                nc.tensor.matmul(out[:, 0:T], a.xs_tok[:, 0, h * HD:(h + 1) * HD], a.mix[:, h % 2, 0:T], start=True, stop=False,
                                 skip_group_check=True)
                nc.tensor.matmul(out[:, P:T], a.xs_tok[:, 1, h * HD:(h + 1) * HD], a.mix[:, h % 2, T:W3], start=False, stop=True,
                                 skip_group_check=True).then_inc(s.values_ready, 1)

            for i in range(SSD_HEADS + 1):
                if i < SSD_HEADS:
                    sums(i)
                if i >= 1:
                    products(i - 1)

        @block.scalar
        def _(act):
            for h in range(SSD_HEADS):
                act.wait_ge(s.scores_ready, h + 1)
                if h >= 2:
                    act.wait_ge(s.probs_ready, h - 1)
                nc.scalar.activation(a.decay[:, h % 2, :], m.ps[h % 4][:, 0:W3], ACT.Exp).then_inc(s.exp_done, 1)



def gla(nc, m, stage, gate_w2):
    s = m.sem
    a = m.a
    NC = T // GLA_CHUNK
    F4 = 4
    chunks = lambda x: x.rearrange("p f (n t) -> p (f n) t", t=GLA_CHUNK)
    wide = lambda col: col.to_broadcast([P, F4 * NC, GLA_CHUNK])
    with stage("gla_decays") as block:
        @block.sync
        def _(sp):
            nc.sync.dma_start(a.w2[:], gate_w2).then_inc(s.loaded, 16)

        @block.gpsimd
        def _(pool):
            nc.gpsimd.memset(a.carry[:], 1.0).then_inc(s.first, 1)
            pool.wait_ge(s.first, 1)
            nc.gpsimd.memset(a.carry[:].rearrange("p (n t) -> p n t", t=GLA_CHUNK)[:, :, 0:1], 0.0).then_inc(s.masked, 1)

        @block.tensor
        def _(pe):
            pe.wait_ge(s.loaded, 16)
            for f in range(F4):
                last = nc.tensor.matmul(m.ps[f // 2][:, (f % 2) * T:(f % 2 + 1) * T], a.w2[:, f * P:(f + 1) * P], a.lr[:],
                                        start=True, stop=True)
            last.then_inc(s.pe_done, 1)
            for n in range(2):
                pe.wait_ge(s.weighted, 1)
                for f in range(F4):
                    last = nc.tensor.transpose(m.ps[2 + n][:, f * P:(f + 1) * P], a.k_end[:, f, n * P:(n + 1) * P], m.ident[:])
                last.then_inc(s.turned, 1)

        @block.vector
        def _(dve):
            link = chain(dve, s.dve_step)
            dve.wait_ge(s.pe_done, 1)
            for f in range(F4):
                link(nc.vector.tensor_scalar(a.gl[:, f, :], m.ps[f // 2][:, (f % 2) * T:(f % 2 + 1) * T],
                                             m.vecs[:, m.v_gate_b + f:m.v_gate_b + f + 1], None, ALU.add))
            nc.vector.scalar_tensor_tensor(out=a.g_abs[:], in0=a.gl[:], scalar=-1.0, in1=a.gl[:], op0=ALU.mult, op1=ALU.max).then_inc(s.abs_ready, 1)
            dve.wait_ge(s.log_ready, 1)
            link(nc.vector.scalar_tensor_tensor(out=a.gl[:], in0=a.gl[:], scalar=0.0, in1=a.g_ln[:], op0=ALU.min, op1=ALU.subtract))
            link(nc.vector.tensor_scalar(a.gl[:], a.gl[:], 1.0 / GLA_NORMALIZER, None, ALU.mult))
            dve.wait_ge(s.masked, 1)
            for f in range(F4):
                last = nc.vector.tensor_tensor_scan(a.gcs[:, f, :], a.carry[:], a.gl[:, f, :], 0.0, ALU.mult, ALU.add)
            link(last)
            g = chunks(a.gcs[:])
            mid, end = g[:, :, GLA_CHUNK // 2:GLA_CHUNK // 2 + 1], g[:, :, GLA_CHUNK - 1:GLA_CHUNK]
            nc.vector.tensor_tensor(chunks(a.to_mid[:]), g, wide(mid), ALU.subtract).then_inc(s.dve_done, 1)
            nc.vector.tensor_tensor(chunks(a.to_end[:]), g, wide(end), ALU.subtract).then_inc(s.dve_done, 1)
            for e, dst, x in ((1, a.q_mid, a.q_fm), (2, a.k_mid, a.k_fm), (3, a.q_start, a.q_fm), (4, a.k_end, a.k_fm)):
                dve.wait_ge(s.exp_done, e)
                last = nc.vector.tensor_tensor(dst[:], dst[:], x[:], ALU.mult)
            last.then_inc(s.weighted, 1)
            for n in range(2):
                dve.wait_ge(s.turned, n + 1)
                nc.vector.tensor_copy(a.k_end_tok[:, n, :], m.ps[2 + n][:])

        @block.scalar
        def _(act):
            act.wait_ge(s.abs_ready, 1)
            nc.scalar.activation(a.g_exp[:], a.g_abs[:], ACT.Exp, scale=-1.0).then_inc(s.act_done, 1)
            act.wait_ge(s.act_done, 1)
            nc.scalar.activation(a.g_ln[:], a.g_exp[:], ACT.Ln, bias=1.0).then_inc(s.log_ready, 1)
            act.wait_ge(s.dve_done, 1)
            nc.scalar.activation(a.q_mid[:], a.to_mid[:], ACT.Exp).then_inc(s.exp_done, 1)
            nc.scalar.activation(a.k_mid[:], a.to_mid[:], ACT.Exp, scale=-1.0).then_inc(s.exp_done, 1)
            nc.scalar.activation(a.q_start[:], a.gcs[:], ACT.Exp).then_inc(s.exp_done, 1)
            act.wait_ge(s.dve_done, 2)
            nc.scalar.activation(a.k_end[:], a.to_end[:], ACT.Exp, scale=-1.0).then_inc(s.exp_done, 1)
            nc.scalar.activation(a.g_chunk[:], chunks(a.gcs[:])[:, :, GLA_CHUNK - 1:GLA_CHUNK].rearrange("p g o -> p (g o)"), ACT.Exp)

    with stage("gla_states") as block:
        @block.tensor
        def _(pe):
            for n in range(NC - 1):
                r = slice(GLA_CHUNK * (n % 2), GLA_CHUNK * (n % 2 + 1))
                if n >= 2:
                    pe.wait_ge(s.dve_done, F4 * (n - 1))
                for f in range(F4):
                    bank = m.ps[4 * (n % 2) + f]
                    for x in range(2):
                        h = 2 * f + x
                        last = nc.tensor.matmul(bank[HD * x:HD * (x + 1), 0:P],
                                                a.k_end_tok[r, n // 2, h * HD:(h + 1) * HD], a.v_tok[r, n // 2, h * P:(h + 1) * P],
                                                start=True, stop=True)
                    last.then_inc(s.pe_done, 1)

        @block.vector
        def _(dve):
            for n in range(NC - 1):
                for f in range(F4):
                    dve.wait_ge(s.pe_done, n * F4 + f + 1)
                    own = m.ps[4 * (n % 2) + f][:, 0:P]
                    if n == 0:
                        nc.vector.tensor_copy(a.state[:, 1, f, :], own).then_inc(s.dve_done, 1)
                    else:
                        dve.wait_ge(s.dve_done, (n - 1) * F4 + f + 1)
                        nc.vector.scalar_tensor_tensor(out=a.state[:, n + 1, f, :], in0=a.state[:, n, f, :],
                                                       scalar=a.g_chunk[:, f * NC + n:f * NC + n + 1], in1=own,
                                                       op0=ALU.mult, op1=ALU.add).then_inc(s.dve_done, 1)

    with stage("gla_out") as block:
        @block.tensor
        def _(pe):
            def scores(h):
                lo, f = HD * (h % 2), h // 2
                if h >= 2:
                    pe.wait_ge(s.masked, h - 1)
                for n in range(NC):
                    t = slice(n * GLA_CHUNK, (n + 1) * GLA_CHUNK)
                    last = nc.tensor.matmul(m.ps[h % 2][GLA_CHUNK * (n % 2):GLA_CHUNK * (n % 2 + 1), (n // 2) * GLA_CHUNK:(n // 2 + 1) * GLA_CHUNK],
                                            a.k_mid[lo:lo + HD, f, t], a.q_mid[lo:lo + HD, f, t], start=True, stop=True)
                last.then_inc(s.scores_ready, 1)

            def out(h):
                lo, f = HD * (h % 2), h // 2
                pe.wait_ge(s.masked, h + 1)
                if h >= 3:
                    pe.wait_ge(s.dve_done, h - 2)
                for n in range(NC):
                    r = slice(GLA_CHUNK * (n % 2), GLA_CHUNK * (n % 2 + 1))
                    t = slice(n * GLA_CHUNK, (n + 1) * GLA_CHUNK)
                    same = n % 2 == h % 2
                    main, other = m.ps[2 + 2 * (h % 3)][:, t], m.ps[3 + 2 * (h % 3)][:, t]
                    last = nc.tensor.matmul(main if same else other, a.v_tok[r, n // 2, h * P:(h + 1) * P],
                                            a.intra[r, h % 2, n // 2, :], start=True, stop=not (same and n))
                    if n:
                        last = nc.tensor.matmul(main, a.state[lo:lo + HD, n, f, :], a.q_start[lo:lo + HD, f, t],
                                                start=not same, stop=True)
                last.then_inc(s.values_ready, 1)

            for i in range(HEADS + 1):
                if i < HEADS:
                    scores(i)
                if i >= 1:
                    out(i - 1)

        @block.vector
        def _(dve):
            def mask(h):
                dve.wait_ge(s.scores_ready, h + 1)
                if h >= 2:
                    dve.wait_ge(s.values_ready, h - 1)
                for x in range(2):
                    r = slice(GLA_CHUNK * x, GLA_CHUNK * (x + 1))
                    upto = m.upto3[r, 0:1, GLA_CHUNK * x:GLA_CHUNK * (x + 1)].to_broadcast([GLA_CHUNK, 2, GLA_CHUNK])
                    last = nc.vector.tensor_tensor(a.intra[r, h % 2, :, :],
                                                   m.ps[h % 2][r, 0:2 * GLA_CHUNK].rearrange("p (n i) -> p n i", n=2), upto, ALU.mult)
                last.then_inc(s.masked, 1)

            def out(h):
                dve.wait_ge(s.act_done, h + 1)
                main, other = a.ob[:, h, :], m.ps[3 + 2 * (h % 3)]
                part = lambda n: slice(n * GLA_CHUNK, (n + 1) * GLA_CHUNK)
                if h % 2:
                    nc.vector.tensor_copy(main[:, part(0)], other[:, part(0)])
                    last = nc.vector.tensor_tensor(main[:, part(2)], main[:, part(2)], other[:, part(2)], ALU.add)
                else:
                    nc.vector.tensor_tensor(main[:, part(1)], main[:, part(1)], other[:, part(1)], ALU.add)
                    last = nc.vector.tensor_tensor(main[:, part(3)], main[:, part(3)], other[:, part(3)], ALU.add)
                last.then_inc(s.dve_done, 1)

            for i in range(HEADS + 1):
                if i < HEADS:
                    mask(i)
                if i >= 1:
                    out(i - 1)

        @block.scalar
        def _(act):
            for h in range(HEADS):
                act.wait_ge(s.values_ready, h + 1)
                first = GLA_CHUNK * (h % 2)
                nc.scalar.activation(a.ob[:, h, first:T], m.ps[2 + 2 * (h % 3)][:, first:T], ACT.Copy).then_inc(s.act_done, 1)


def multiply(nc, m, stage, name, dst, other):
    with stage(name) as block:
        @block.vector
        def _(dve):
            nc.vector.tensor_tensor(dst[:], dst[:], other[:], ALU.mult)



def moba(nc, m, stage):
    s = m.sem
    a = m.a
    units = [(h, t) for h in range(MOBA_HEADS) for t in range(TT)]
    N = len(units)
    with stage("moba") as block:
        @block.tensor
        def _(pe):
            def scores(u):
                h, t = units[u]
                lo, c = HD * (h % 2), h // 2
                if u >= 4:
                    pe.wait_ge(s.capped, u - 3)
                keys = (t + 1) * P
                nc.tensor.matmul(m.ps[u % 4][:, 0:keys], a.mq[lo:lo + HD, c, t * P:(t + 1) * P], a.mk[lo:lo + HD, c, 0:keys],
                                 start=True, stop=True).then_inc(s.scores_ready, 1)

            def turn(u):
                h, t = units[u]
                pe.wait_ge(s.weighted, u + 1)
                if u >= 2:
                    pe.wait_ge(s.turned, u - 1)
                for k in range(t + 1):
                    last = nc.tensor.transpose(m.ps[4 + u % 2][:, k * P:(k + 1) * P], a.mp[:, u % 4, k * P:(k + 1) * P], m.ident[:])
                last.then_inc(s.pe_done, 1)

            def values(u):
                h, t = units[u]
                pe.wait_ge(s.turned, u + 1)
                lo, bank = HD * (h % 2), m.ps[6 + (h // 2) % 2]
                if h >= 4 and h % 2 == 0 and t == 0:
                    pe.wait_ge(s.dve_done, h // 2 - 1)
                for k in range(t + 1):
                    last = nc.tensor.matmul(bank[lo:lo + HD, t * P:(t + 1) * P], a.mv[:, k, h * HD:(h + 1) * HD],
                                            a.mp_t[:, u % 2, k * P:(k + 1) * P], start=(k == 0), stop=(k == t))
                last.then_inc(s.values_ready, 1)

            for i in range(N + 3):
                if i < N:
                    scores(i)
                if 2 <= i < N + 2:
                    turn(i - 2)
                if i >= 3:
                    values(i - 3)

        @block.vector
        def _(dve):
            link = chain(dve, s.dve_step)

            def cap(u):
                h, t = units[u]
                keys = (t + 1) * P
                dve.wait_ge(s.scores_ready, u + 1)
                if u >= 2:
                    dve.wait_ge(s.exp_done, u - 1)
                diag = slice(t * P, keys)
                if t:
                    nc.vector.tensor_copy(a.ms[:, u % 2, 0:P], m.ps[u % 4][:, 0:P])
                link(nc.vector.tensor_tensor(a.ms[:, u % 2, diag], m.ps[u % 4][:, diag], a.causal[:], ALU.min))
                nc.vector.tensor_reduce(a.neg_max[:, u:u + 1], a.ms[:, u % 2, 0:keys], AX_X, ALU.max, negate=True
                                        ).then_inc(s.capped, 1)

            def weigh(u):
                h, t = units[u]
                keys = (t + 1) * P
                dve.wait_ge(s.exp_done, u + 1)
                link(nc.vector.reciprocal(a.rec[:, u:u + 1], a.sums[:, u:u + 1]))
                nc.vector.tensor_scalar(a.mp[:, u % 4, 0:keys], a.mp[:, u % 4, 0:keys], a.rec[:, u:u + 1], None, ALU.mult
                                        ).then_inc(s.weighted, 1)

            def out(c):
                dve.wait_ge(s.values_ready, 4 * (c + 1))
                nc.vector.tensor_tensor(a.my[:, c, :], m.ps[6 + c % 2][:, 0:T], a.mz[:, c, :], ALU.mult).then_inc(s.dve_done, 1)

            for i in range(N + 4):
                if i < N:
                    cap(i)
                if 1 <= i < N + 1:
                    weigh(i - 1)
                if i >= 4 and (i - 4) % 4 == 3:
                    out((i - 4) // 4)

        @block.scalar
        def _(act):
            def exps(u):
                h, t = units[u]
                keys = (t + 1) * P
                act.wait_ge(s.capped, u + 1)
                if u >= 4:
                    act.wait_ge(s.pe_done, u - 3)
                nc.scalar.activation(a.mp[:, u % 4, 0:keys], a.ms[:, u % 2, 0:keys], ACT.Exp, bias=a.neg_max[:, u:u + 1],
                                     accum_out=a.sums[:, u:u + 1]).then_inc(s.exp_done, 1)

            def copy(u):
                h, t = units[u]
                keys = (t + 1) * P
                act.wait_ge(s.pe_done, u + 1)
                if u >= 2:
                    act.wait_ge(s.values_ready, u - 1)
                nc.scalar.activation(a.mp_t[:, u % 2, 0:keys], m.ps[4 + u % 2][:, 0:keys], ACT.Copy).then_inc(s.turned, 1)

            for i in range(N + 2):
                if i < N:
                    exps(i)
                if i >= 2:
                    copy(i - 2)



def allocate(nc, ctx):
    m = Names()

    def sb(name, shape, dt=F32):
        return ctx.enter_context(nc.sbuf_tensor(name, shape, dt))

    m.ps = [ctx.enter_context(nc.psum_tensor(f"bank{i}", [P, BANK], F32)) for i in range(8)]
    m.x_fm = sb("x_fm", [P, C, T])
    m.h_fm = sb("h_fm", [P, C, T])
    m.h_tok = sb("h_tok", [P, TT, D])
    m.x_tok = m.h_tok
    m.dots = sb("dots", [P, TT, HK])
    m.gate = sb("gate", [P, TT, HK])
    m.expert = sb("expert", [P, TT, HK], U32)
    m.key1_t = sb("key1_t", [P, T])
    m.key2_t = sb("key2_t", [P, T])
    m.weight_t = sb("weight_t", [P, T])
    m.index = [sb(f"index{u}", [P, GSLOTS], U32) for u in range(TOPK // GSLOTS)]
    m.layer_base = sb("layer_base", [P, 1])
    m.ident = sb("ident", [P, P])
    m.ones = sb("ones", [P, P])
    m.neg_ones = sb("neg_ones", [P, P])
    m.neg_tri = sb("neg_tri", [P, P])
    m.after = sb("after", [P, P])
    m.count = sb("count", [P, P])
    m.keep3 = sb("keep3", [P, 3, P])
    m.cap3 = sb("cap3", [P, 3, P])
    m.upto3 = sb("upto3", [P, 3, P])
    m.zeros_bf = sb("zeros_bf", [P, BANK], BF16)
    m.vec_rows = sb("vec_rows", [P, P])
    m.vecs = sb("vecs", [P, P])
    m.mod = sb("mod", [P, 6 * C])
    m.gain = sb("gain", [P, 2 * C])
    m.c_rows = sb("c_rows", [C, P])
    m.c_act = sb("c_act", [P, C])

    hot = m.h_fm[:].rearrange("p c t -> p (c t)")
    m.hot1 = hot[:, 0:D].rearrange("p (b k i) -> p b k i", b=2, k=4)
    m.hot2 = hot[:, D:2 * D].rearrange("p (b k i) -> p b k i", b=2, k=4)

    m.stream = sb("stream", [P, GSLOTS * D])
    m.rows = [m.stream[:, g * D:(g + 1) * D] for g in range(GSLOTS)]
    m.value_ring = [m.stream[:, n * VJ * D:(n + 1) * VJ * D] for n in range(VSLOTS)]
    part = lambda n: m.stream[:, n * C * T:(n + 1) * C * T].rearrange("p (c t) -> p c t", c=C)
    m.squares, m.mean, m.root, m.rstd = (part(n) for n in range(4))

    m.arena = sb("arena", [P, KEYS * T])
    m.weights = m.arena[:].rearrange("p (j t) -> p j t", j=KEYS)
    slot = 8 * GROUP
    end = KEYS * T
    m.weight_ring = [m.stream[:, 0:slot], m.stream[:, slot:2 * slot], m.arena[:, end - slot:end], m.arena[:, end - 2 * slot:end - slot]]
    m.arena_end = end - 2 * slot

    sems = ["loaded", "stored", "slot_free", "pe_done", "act_done", "dve_done", "first", "masked", "normed", "dve_step",
            "pool_step", "mean_ready", "root_ready", "scaled", "scores_ready", "capped", "sp_ready", "logs_ready", "probs_ready",
            "values_ready", "abs_ready", "exp_done", "log_ready", "index_ready", "weighted", "turned", "quads_placed",
            "hot_ready", "spread", "gathers_started"]
    named = {name: nc.alloc_semaphore(name) for name in sems}
    handles = list(named.values())
    m.sem = Names(**named)
    m.sem.slot_loaded = [nc.alloc_semaphore(f"slot_loaded{g}") for g in range(GSLOTS)]
    handles += m.sem.slot_loaded
    nums = sorted(h.num for h in handles)
    assert nums == list(range(nums[0], nums[-1] + 1))
    m.to_clear = range(nums[0], nums[-1] + 1)
    m.sem.rows_loaded = [nc.alloc_semaphore(f"rows_loaded{g}") for g in range(GSLOTS)]
    return m


def carve(m, plan):
    views = {}
    at = 0
    for name, (shape, dt) in plan.items():
        size = 1
        for n in shape:
            size *= n
        assert at + size <= m.arena_end, name
        v = m.arena[:, at:at + size]
        at += size
        if dt is not F32:
            v = v.bitcast(dt)
        if len(shape) == 2:
            v = v.rearrange("p (a b) -> p a b", a=shape[0])
        elif len(shape) == 3:
            v = v.rearrange("p (a b c) -> p a b c", a=shape[0], b=shape[1])
        views[name] = v
    return Names(**views)


def columns(w, start, count):
    return w[:, start:start + count]


def rows_of(v):
    return v.rearrange("(r p) -> r p", p=P)


def first_block(nc, m, stage, d, layer):
    at = lambda name: d[name][bass.ds(layer, 1)]
    one = lambda name, pattern, **k: at(name).rearrange(pattern, **k)
    load_vectors(nc, m, stage, "vectors1", [
        (one("ada_b", "l (r p) -> (l r) p", p=P), 6 * C), (one("norm_mix", "l (r p) -> (l r) p", p=P), C),
        (one("norm_ffn", "l (r p) -> (l r) p", p=P), C), (one("out_norm_a", "l (r p) -> (l r) p", p=P), 4),
        (one("out_norm_b", "l (r p) -> (l r) p", p=P), 4)], m.vecs)
    modulation(nc, m, stage, one("ada_w", "l k n -> (l k) n"), d["c"].rearrange("o (r p) -> (o r) p", p=P), m.weight_ring)
    chunk = lambda i: m.mod[:, i * C:(i + 1) * C]

    norm(nc, m, stage, "norm1", m.x_fm, m.h_fm, C, m.gain[:, 0:C], chunk(0))
    a = m.a = carve(m, {
        "y": ([C, T], F32), "u_gelu": ([4, T], F32), "v_gelu": ([TT, 512], F32), "q_fm": ([4, T], F32), "k_fm": ([4, T], F32),
        "v_tok": ([TT, 512], F32), "v_sq": ([TT, 512], F32), "v_norm": ([TT, 512], F32), "gain_row": ([512], F32),
        "ws": ([HEADS, P], F32), "ws_t": ([HEADS, P], F32), "bias_row": ([HEADS * P], F32),
        "v_mean": ([16], F32), "v_root": ([16], F32), "v_rstd": ([16], F32),
        "absz": ([2, 384], F32), "expz": ([2, 384], F32), "lnp": ([2, 384], F32), "sp": ([2, 384], F32),
        "loga": ([2, 384], F32), "probs": ([2, 384], F32)})
    a.bias_row = a.bias_row[0:1, :]
    w = one("w_in", "l k n -> (l k) n")
    G = GROUP
    project(nc, m, stage, "in1", m.h_fm, C, [
        (columns(w, 0, G), "feature", [act_fn(nc, a.u_gelu[:, 2 * u:2 * u + 2, :], ACT.Gelu_apprx_tanh) for u in range(2)]),
        (columns(w, G, G), "token", [act_fn(nc, a.v_gelu[:, t, :], ACT.Gelu_apprx_tanh) for t in range(2)]),
        (columns(w, 2 * G, G), "feature", [act_fn(nc, a.q_fm[:, 2 * u:2 * u + 2, :], ACT.Copy, scale=HD ** -0.5) for u in range(2)]),
        (columns(w, 3 * G, G), "feature", [dve_copy(nc, a.k_fm[:, 2 * u:2 * u + 2, :]) for u in range(2)]),
        (columns(w, 4 * G, G), "token", [dve_copy(nc, a.v_tok[:, t, :]) for t in range(2)])], m.weight_ring)
    gmlp(nc, m, stage, one("gm_ws", "l h t s -> (l h) t s"), one("gm_bs", "l h t -> (l h) t"), at("gm_vnorm"))
    stick_breaking(nc, m, stage)
    norm(nc, m, stage, "norm_y", a.y, m.h_fm, C, m.vecs[:, 8 * C:9 * C], width=4)
    w = one("w_out", "l k n -> (l k) n")
    project(nc, m, stage, "out1", m.h_fm, C, [
        (columns(w, n * G, G), "feature", [residual(nc, m, 4 * n + 2 * u, chunk(2)) for u in range(2)]) for n in range(2)], m.weight_ring)

    norm(nc, m, stage, "norm2", m.x_fm, m.h_fm, C, m.gain[:, C:2 * C], chunk(3))
    to_token_major(nc, m, stage, "h_token", m.h_fm, m.h_tok)
    a = m.a = carve(m, {
        "query": ([2 * C, T], F32), "key_table": ([2, P], F32), "keys_t": ([2, P], F32),
        "scores": ([32, KEYS], F32), "spare": ([32, KEYS], F32), "best": ([32, TOPK], F32), "where": ([32, TOPK], U32),
        "key_no": ([32, TOPK], F32), "top": ([16, TOPK], F32), "place": ([16, TOPK], U32),
        "place_ij": ([2, 16, TOPK], U32), "place_no": ([2, 16, TOPK], F32), "gate": ([16, TOPK], F32),
        "gate_sum": ([16], F32), "gate_rec": ([16], F32), "chosen": ([2, TT, HK], F32), "number": ([TT, HK], F32),
        "hits": ([HK, TOPK], F32), "pairs": ([16, 256], F32)})
    a.pair_spare = a.scores.rearrange("p a b -> p (a b)").rearrange("p (g n) -> p g n", g=16)
    w = one("peer_wq", "l k n -> (l k) n")
    project(nc, m, stage, "query", m.h_fm, C, [
        (columns(w, n * G, G), "feature",
         [(act_fn(nc, a.query[:, 4 * n + 2 * u:4 * n + 2 * u + 2, :], ACT.Copy) if u else
           dve_copy(nc, a.query[:, 4 * n + 2 * u:4 * n + 2 * u + 2, :])) for u in range(2)]) for n in range(4)], m.weight_ring)
    router(nc, m, stage, one("peer_k1", "l k n -> (l k) n"), one("peer_k2", "l k n -> (l k) n"))
    experts(nc, m, stage, d["peer_u"].rearrange("l e n -> (l e) n"), layer)
    expert_values(nc, m, stage, one("peer_v", "l e n -> (l e) n"), chunk(5), m.value_ring)


def second_block(nc, m, stage, d, out):
    flat = lambda name: d[name].rearrange("l n -> (l n)")
    m.v_norm, m.v_conv, m.v_conv_b, m.v_ssd, m.v_gate_b, m.v_gla, m.v_odd, m.v_final = 0, 8, 48, 58, 66, 70, 78, 86
    load_vectors(nc, m, stage, "vectors2", [
        (rows_of(flat("even_norm_2")), 8), (d["even_conv_w_2"].rearrange("l k (r p) -> (l k r) p", p=P), 40),
        (rows_of(flat("even_conv_b_2")), 10), (rows_of(flat("even_ssd_norm_2")), 8), (rows_of(flat("even_gate_b_2")), 4),
        (d["even_gla_norm_2"].to_broadcast([8, P]), 8), (rows_of(flat("odd_norm_2")), 8), (rows_of(d["final_norm_2"]), 8)], m.vecs)
    vec = lambda start, n=C: m.vecs[:, start:start + n]

    norm(nc, m, stage, "norm3", m.x_fm, m.h_fm, C, vec(m.v_norm))
    a = m.a = carve(m, {
        "z_silu": ([C, T], F32), "xbc": ([XBC, T + CONV - 1], F32), "q_fm": ([4, T], F32), "k_fm": ([4, T], F32),
        "v_tok": ([TT, D], F32), "g_silu": ([C, T], F32), "lr": ([T], F32), "dt_raw": ([TT, SSD_HEADS], F32),
        "conv": ([XBC, T], F32),
        "dt_row": ([16], F32), "a_row": ([16], F32), "a_exp": ([16], F32), "d_col": ([C], F32),
        "dt": ([TT, 16], F32), "dt_abs": ([TT, 16], F32), "dt_exp": ([TT, 16], F32), "dt_ln": ([TT, 16], F32), "dta": ([TT, 16], F32),
        "work": ([8800], F32)})
    work, at = a.work, [0]

    def take(*shape):
        size = 1
        for n in shape:
            size *= n
        v = work[:, at[0]:at[0] + size]
        at[0] += size
        assert at[0] <= 8800
        if len(shape) == 2:
            return v.rearrange("p (a b) -> p a b", a=shape[0])
        if len(shape) == 3:
            return v.rearrange("p (a b c) -> p a b c", a=shape[0], b=shape[1])
        return v

    y = m.h_tok[:].rearrange("p t d -> p (t d)").rearrange("p (c t) -> p c t", c=C)
    a.ya, a.ob = y, None
    a.xs_tok, a.cb = take(TT, D), take(2, 384)
    a.steps, a.decay, a.mix = take(2, 3, P), take(2, 384), take(2, 384)
    a.lr = a.lr[0:16, :]
    w = d["even_w_in_2"].rearrange("l k n -> (l k) n")
    G = GROUP
    o_x, o_dt, o_q, o_k, o_v, o_lr, o_g = 1024, 2304, 2320, 2832, 3344, 4368, 4384
    xbc = lambda c: a.xbc[:, c:c + 2, CONV - 1:]
    project(nc, m, stage, "in2", m.h_fm, C, [
        (columns(w, o_x + n * G, G if n < 2 else 256), "feature", [dve_copy(nc, xbc(4 * n + 2 * u)) for u in range(2 if n < 2 else 1)])
        for n in range(3)] + [
        (columns(w, n * G, G), "feature", [act_fn(nc, a.z_silu[:, 4 * n + 2 * u:4 * n + 2 * u + 2, :], ACT.Silu) for u in range(2)])
        for n in range(2)] + [
        (columns(w, o_dt, 16), "token", [dve_copy(nc, a.dt_raw[:, t, :]) for t in range(2)]),
        (columns(w, o_q, G), "feature", [act_fn(nc, a.q_fm[:, 2 * u:2 * u + 2, :], ACT.Copy, scale=HD ** -0.5) for u in range(2)]),
        (columns(w, o_k, G), "feature", [dve_copy(nc, a.k_fm[:, 2 * u:2 * u + 2, :]) for u in range(2)]),
        (columns(w, o_v, G), "token", [dve_copy(nc, a.v_tok[:, t, 0:G]) for t in range(2)]),
        (columns(w, o_v + G, G), "token", [dve_copy(nc, a.v_tok[:, t, G:2 * G]) for t in range(2)]),
        (columns(w, o_lr, 16), "feature", [dve_copy(nc, a.lr[:, :])])] + [
        (columns(w, o_g + n * G, G), "feature", [act_fn(nc, a.g_silu[:, 4 * n + 2 * u:4 * n + 2 * u + 2, :], ACT.Silu) for u in range(2)])
        for n in range(2)], m.weight_ring)
    convolve(nc, m, stage)
    ssd(nc, m, stage, d["even_a_log_2"], d["even_dt_bias_2"], d["even_d_skip_2"])
    both = carve(m, {"z": ([C, T], F32)})
    a.concat = m.arena[:, 0:2 * C * T].rearrange("p (c t) -> p c t", c=2 * C)
    a.ya_out = m.h_fm
    norm(nc, m, stage, "norm_ssd", a.ya, m.h_fm, C, vec(m.v_ssd))

    at[0] = 0
    a.gl, a.gcs, a.q_mid, a.k_mid, a.q_start, a.k_end = (take(4, T) for _ in range(6))
    a.k_end_tok = take(TT, 512)
    a.g_chunk, a.carry = take(16), take(T)
    a.w2 = take(512)[0:16, :]
    a.intra = take(2, 2, GLA_CHUNK)
    free = m.arena[:, 0:4600]
    piece = lambda n: free[:, n * 1024:(n + 1) * 1024].rearrange("p (f t) -> p f t", f=4)
    a.to_mid, a.to_end, a.g_ln, a.g_exp = (piece(n) for n in range(4))
    a.g_abs = a.to_mid
    a.state = a.conv.rearrange("p c t -> p (c t)")[:, 0:4 * 512].rearrange("p (n f v) -> p n f v", n=4, f=4)
    a.ob = y
    gla(nc, m, stage, d["even_gate_w2_2"].rearrange("l r n -> (l r) n"))
    norm(nc, m, stage, "norm_gla", a.ob, a.ob, C, vec(m.v_gla), width=1)
    multiply(nc, m, stage, "gate_gla", a.ob, a.g_silu)
    w = d["even_w_out_2"].rearrange("l k n -> (l k) n")
    both = TwoHalves(m.h_fm, a.ob)
    project(nc, m, stage, "out2", both, 2 * C, [
        (columns(w, n * 256, 256), "feature", [residual(nc, m, 2 * n, None)]) for n in range(4)], m.weight_ring)

    norm(nc, m, stage, "norm4", m.x_fm, m.h_fm, C, vec(m.v_odd))
    a = m.a = carve(m, {
        "mq": ([C, T], F32), "mk": ([C, T], F32), "mv": ([TT, D], F32), "mz": ([C, T], F32), "my": ([C, T], F32),
        "ms": ([2, T], F32), "mp": ([4, T], F32), "mp_t": ([2, T], F32), "neg_max": ([32], F32), "sums": ([32], F32),
        "rec": ([32], F32), "causal": ([P], F32)})
    w = d["odd_w_in_2"].rearrange("l k n -> (l k) n")
    project(nc, m, stage, "in3", m.h_fm, C, [
        (columns(w, n * G, G), "feature", [act_fn(nc, a.mq[:, 4 * n + 2 * u:4 * n + 2 * u + 2, :], ACT.Copy, scale=HD ** -0.5) for u in range(2)])
        for n in range(2)] + [
        (columns(w, D + n * G, G), "feature", [dve_copy(nc, a.mk[:, 4 * n + 2 * u:4 * n + 2 * u + 2, :]) for u in range(2)])
        for n in range(2)] + [
        (columns(w, 2 * D + n * G, G), "token", [dve_copy(nc, a.mv[:, t, n * G:(n + 1) * G]) for t in range(2)])
        for n in range(2)] + [
        (columns(w, 3 * D + n * G, G), "feature", [act_fn(nc, a.mz[:, 4 * n + 2 * u:4 * n + 2 * u + 2, :], ACT.Silu) for u in range(2)])
        for n in range(2)], m.weight_ring)
    causal_mask(nc, m, stage)
    moba(nc, m, stage)
    w = d["odd_w_out_2"].rearrange("l k n -> (l k) n")
    project(nc, m, stage, "out3", a.my, C, [
        (columns(w, n * G, G), "feature", [residual(nc, m, 4 * n + 2 * u, None) for u in range(2)]) for n in range(2)], m.weight_ring)
    norm(nc, m, stage, "norm5", m.x_fm, m.h_fm, C, vec(m.v_final))
    to_token_major(nc, m, stage, "out_token", m.h_fm, m.h_tok, store=out.rearrange("o t d -> (o t) d"))


class TwoHalves:

    def __init__(self, first, second):
        self.parts = (first, second)

    def __getitem__(self, key):
        p, k, t = key
        return self.parts[k // C][p, k % C, t]


def causal_mask(nc, m, stage):
    s = m.sem
    with stage("causal") as block:
        @block.gpsimd
        def _(pool):
            nc.gpsimd.memset(m.a.causal[:], -NEG).then_inc(s.first, 1)
            pool.wait_ge(s.first, 1)
            nc.gpsimd.affine_select(out=m.a.causal[:], in_=m.a.causal[:], compare_op=ALU.is_ge, fill=-1.0e30,
                                    base=0, pattern=[[-1, P]], channel_multiplier=1)


def program(nc, d, out):
    with ExitStack() as ctx:
        m = allocate(nc, ctx)
        m.x_dram = d["x"]
        stage = stage_maker(nc, m.to_clear)
        make_constants(nc, m, stage)
        to_feature_major(nc, m, stage, "x_feature", m.x_tok, m.x_fm)
        with nc.Fori(0, DEPTH) as layer:
            first_block(nc, m, stage, d, layer)
        load_vectors(nc, m, stage, "vectors_final", [(rows_of(d["final_norm"]), C)], m.vecs)
        norm(nc, m, stage, "norm_final", m.x_fm, m.x_fm, C, m.vecs[:, 0:C])
        second_block(nc, m, stage, d, out)


_INS = ["x", "c", "ada_w", "ada_b", "norm_mix", "norm_ffn", "w_in", "gm_ws", "gm_bs", "gm_vnorm", "out_norm_a", "out_norm_b",
        "w_out", "peer_wq", "peer_k1", "peer_k2", "peer_u", "peer_v", "final_norm", "even_norm_2", "even_w_in_2",
        "even_conv_w_2", "even_conv_b_2", "even_a_log_2", "even_dt_bias_2", "even_d_skip_2", "even_ssd_norm_2",
        "even_gate_w2_2", "even_gate_b_2", "even_gla_norm_2", "even_w_out_2", "odd_norm_2", "odd_w_in_2", "odd_w_out_2",
        "final_norm_2"]


def kernel(**inputs):
    import numpy as np
    import concourse.bacc as bacc
    from concourse.bass_utils import run_bass_kernel_spmd

    nc = bacc.Bacc("TRN2", target_bir_lowering=False, num_devices=1)
    arrays, d = {}, {}
    for name in _INS:
        x = np.ascontiguousarray(inputs[name])
        arrays[f"in_{name}"] = x
        d[name] = nc.dram_tensor(f"in_{name}", x.shape, mybir.dt.from_np(x.dtype), kind="ExternalInput").ap()
    out = nc.dram_tensor("out", (1, T, D), F32, kind="ExternalOutput").ap()
    program(nc, d, out)
    r = run_bass_kernel_spmd(nc, [arrays], core_ids=[0])
    return r.results[0]["out"]
```

```python
from contextlib import ExitStack, contextmanager

import concourse.bass as bass
from concourse import mybir

F32 = mybir.dt.float32
BF16 = mybir.dt.bfloat16
U32 = mybir.dt.uint32
ALU = mybir.AluOpType
ACT = mybir.ActivationFunctionType
AX_X = mybir.AxisListType.X

P = 128
T = 256
TT = T // P
D = 1024
C = D // P
DEPTH = 2
EPS = 1e-6
GROUP = 512
BANK = 512

HEADS = 8
HD = 64
TOPK = 16
HK = HEADS * TOPK
KEYS = 128
EXPERTS = KEYS * KEYS
NEG = -3.0e38

GSLOTS = 8
VSLOTS = 4
VJ = 2

SSD_HEADS = 16
XBC = 10
CONV = 4
GLA_CHUNK = 64
GLA_NORMALIZER = 16.0
MOBA_HEADS = 16


class Names(dict):

    def __getattr__(self, name):
        return self[name]

    def __setattr__(self, name, value):
        self[name] = value


def chain(eng, sem):
    count = [0]

    def link(ins):
        count[0] += 1
        ins.then_inc(sem, 1)
        eng.wait_ge(sem, count[0])
    return link


def stage_maker(nc, clear, suffix=""):
    @contextmanager
    def stage(name):
        with nc.Block(name + suffix) as block:
            yield block
        nc.all_engine_barrier(sems_to_clear=clear)
    return stage



def make_constants(nc, m, stage, ahead):
    s = m.sem
    with stage("constants") as block:
        @block.gpsimd
        def _(pool):
            link = chain(pool, s.pool_step)
            nc.gpsimd.memset(m.zeros_bf[:], 0.0)
            nc.gpsimd.memset(m.ident[:], 0.0)
            nc.gpsimd.memset(m.ones[:], 1.0)
            nc.gpsimd.memset(m.neg_ones[:], -1.0)
            nc.gpsimd.memset(m.layer_base[:], 0.0)
            nc.gpsimd.memset(m.keep3[:], 1.0)
            nc.gpsimd.memset(m.cap3[:], 0.0)
            nc.gpsimd.memset(m.upto3[:], 1.0)
            nc.gpsimd.memset(m.after[:], 1.0)
            nc.gpsimd.iota(m.count[:], pattern=[[1, P]], base=0, channel_multiplier=0,
                           allow_small_or_imprecise_dtypes=True)
            link(nc.gpsimd.memset(m.neg_tri[:], -1.0))
            nc.gpsimd.affine_select(out=m.ident[:], in_=m.ident[:], compare_op=ALU.not_equal, fill=1.0,
                                    base=0, pattern=[[-1, P]], channel_multiplier=1)
            nc.gpsimd.affine_select(out=m.neg_tri[:], in_=m.neg_tri[:], compare_op=ALU.is_ge, fill=0.0,
                                    base=0, pattern=[[-1, P]], channel_multiplier=1)
            nc.gpsimd.affine_select(out=m.after[:], in_=m.after[:], compare_op=ALU.is_gt, fill=0.0,
                                    base=0, pattern=[[-1, P]], channel_multiplier=1)
            for b in (0, 2):
                nc.gpsimd.affine_select(out=m.keep3[:, b, :], in_=m.keep3[:, b, :], compare_op=ALU.is_gt, fill=0.0,
                                        base=0, pattern=[[1, P]], channel_multiplier=-1)
                nc.gpsimd.affine_select(out=m.cap3[:, b, :], in_=m.cap3[:, b, :], compare_op=ALU.is_gt, fill=NEG,
                                        base=0, pattern=[[1, P]], channel_multiplier=-1)
                nc.gpsimd.affine_select(out=m.upto3[:, b, :], in_=m.upto3[:, b, :], compare_op=ALU.is_ge, fill=0.0,
                                        base=0, pattern=[[1, P]], channel_multiplier=-1)

        @block.sync
        def _(sp):
            nc.sync.dma_start(m.x_tok[:], m.x_dram.rearrange("o (a p) d -> p (o a) d", p=P)).then_inc(s.loaded, 16)
            start_loads(nc, m, ahead)
            sp.wait_ge(s.loaded, 16)


def to_feature_major(nc, m, stage, name, src, dst):
    s = m.sem
    with stage(name) as block:
        @block.tensor
        def _(pe):
            for n in range(TT * C // 4):
                t, q = n // (C // 4), n % (C // 4)
                for k in range(4):
                    c = 4 * q + k
                    last = nc.tensor.transpose(m.ps[n][:, k * P:(k + 1) * P], src[:, t, c * P:(c + 1) * P], m.ident[:])
                last.then_inc(s.pe_done, 1)

        @block.vector
        def _(dve):
            for n in range(TT * C // 4):
                t, q = n // (C // 4), n % (C // 4)
                dve.wait_ge(s.pe_done, n + 1)
                nc.vector.tensor_copy(dst[:, 4 * q:4 * q + 4, t * P:(t + 1) * P],
                                      m.ps[n][:].rearrange("p (c t) -> p c t", c=4))


def to_token_major(nc, m, stage, name, src, dst, store=None):
    s = m.sem
    with stage(name) as block:
        @block.tensor
        def _(pe):
            for n in range(TT * C // 4):
                t, q = n // (C // 4), n % (C // 4)
                for k in range(4):
                    last = nc.tensor.transpose(m.ps[n][:, k * P:(k + 1) * P],
                                               src[:, 4 * q + k, t * P:(t + 1) * P], m.ident[:])
                last.then_inc(s.pe_done, 1)

        @block.vector
        def _(dve):
            for n in range(TT * C // 4):
                t, q = n // (C // 4), n % (C // 4)
                dve.wait_ge(s.pe_done, n + 1)
                nc.vector.tensor_copy(dst[:, t, q * BANK:(q + 1) * BANK], m.ps[n][:]).then_inc(s.dve_done, 1)

        if store is not None:
            @block.sync
            def _(sp):
                for t in range(TT):
                    sp.wait_ge(s.dve_done, (t + 1) * C // 4)
                    nc.sync.dma_start(store[t * P:(t + 1) * P, :], dst[:, t, :]).then_inc(s.stored, 16)
                sp.wait_ge(s.stored, 16 * TT)


def load_vectors(nc, m, stage, name, rows, dst):
    s = m.sem
    total = sum(n for _, n in rows)
    with stage(name) as block:
        @block.sync
        def _(sp):
            at = 0
            for src, n in rows:
                nc.sync.dma_start(m.vec_rows[at:at + n, :], src).then_inc(s.loaded, 16)
                at += n

        @block.tensor
        def _(pe):
            pe.wait_ge(s.loaded, 16 * len(rows))
            nc.tensor.transpose(m.ps[0][:, 0:total], m.vec_rows[0:total, :], m.ident[0:total, 0:total]).then_inc(s.pe_done, 1)

        @block.vector
        def _(dve):
            dve.wait_ge(s.pe_done, 1)
            nc.vector.tensor_copy(dst[:, 0:total], m.ps[0][:, 0:total])



AHEAD = 2


def start_loads(nc, m, weights):
    m.starts += 1
    for n, w in enumerate(weights[0:AHEAD]):
        kchunks = w.shape[0] // P
        slot = m.weight_ring[n].rearrange("p (k n) -> p k n", k=kchunks)
        nc.sync.dma_start(slot[:, :, 0:w.shape[1]], w.rearrange("(k p) n -> p k n", p=P)).then_inc(m.sem.started[n], 16)


def norm(nc, m, stage, name, src, dst, chunks, gain, shift=None, width=None, ahead=None):
    s = m.sem
    width = width or chunks
    sets = chunks // width
    with stage(name) as block:
        if ahead is not None:
            @block.sync
            def _(sp):
                start_loads(nc, m, ahead)

        @block.scalar
        def _(act):
            for c in range(0, chunks, 2):
                nc.scalar.activation(m.squares[:, c:c + 2, :], src[:, c:c + 2, :], ACT.Square).then_inc(s.act_done, 1)
            for g in range(sets):
                act.wait_ge(s.mean_ready, g + 1)
                nc.scalar.activation(m.root[:, g, :], m.mean[:, g, :], ACT.Sqrt).then_inc(s.root_ready, 1)
            if shift is not None:
                for c in range(chunks):
                    act.wait_ge(s.scaled, c + 1)
                    nc.scalar.activation(dst[:, c, :], dst[:, c, :], ACT.Identity, bias=shift[:, c:c + 1])

        @block.tensor
        def _(pe):
            for g in range(sets):
                for k in range(width):
                    c = g * width + k
                    pe.wait_ge(s.act_done, c // 2 + 1)
                    last = nc.tensor.matmul(m.ps[g][:, 0:T], m.ones[:], m.squares[:, c, :],
                                            start=(k == 0), stop=(k == width - 1))
                last.then_inc(s.pe_done, 1)

        @block.vector
        def _(dve):
            link = chain(dve, s.dve_step)
            for g in range(sets):
                dve.wait_ge(s.pe_done, g + 1)
                nc.vector.tensor_scalar(m.mean[:, g, :], m.ps[g][:, 0:T], 1.0 / (width * P), EPS,
                                        ALU.mult, ALU.add).then_inc(s.mean_ready, 1)
            for g in range(sets):
                dve.wait_ge(s.root_ready, g + 1)
                link(nc.vector.reciprocal(m.rstd[:, g, :], m.root[:, g, :]))
                for k in range(width):
                    c = g * width + k
                    nc.vector.scalar_tensor_tensor(out=dst[:, c, :], in0=src[:, c, :], scalar=gain[:, c:c + 1],
                                                   in1=m.rstd[:, g, :], op0=ALU.mult, op1=ALU.mult).then_inc(s.scaled, 1)



def project(nc, m, stage, name, act_in, kchunks, loads, ring, beside=None):
    s = m.sem
    width = 8 * GROUP // kchunks
    slots = len(ring)
    views = [r[:].rearrange("p (k n) -> p k n", k=kchunks) for r in ring]
    starts = m.starts
    units = []
    for n, (w, kind, evac) in enumerate(loads):
        cols = w.shape[1]
        for u, (engine, fn) in enumerate(evac):
            units.append((n, u, cols, kind, engine, fn))
    by_engine = {e: [i for i, x in enumerate(units) if x[4] == e] for e in ("act", "dve")}
    done_by = {"act": s.act_done, "dve": s.dve_done}

    def view(i):
        n, u, cols, kind, _, _ = units[i]
        bank = m.ps[i % 8]
        if kind == "token":
            return bank[:, 0:cols]
        if cols < P:
            return bank[0:cols, 0:T]
        return bank[:].rearrange("p (c t) -> p c t", c=2)

    with stage(name) as block:
        @block.sync
        def _(sp):
            for n, (w, kind, evac) in enumerate(loads):
                if n < AHEAD:
                    continue
                if n >= slots:
                    sp.wait_ge(s.pe_done, sum(len(x[2]) for x in loads[:n - slots + 1]))
                cols = w.shape[1]
                nc.sync.dma_start(views[n % slots][:, :, 0:cols],
                                  w.rearrange("(k p) n -> p k n", p=P)).then_inc(s.slot_loaded[n % slots], 16)

        @block.tensor
        def _(pe):
            for i, (n, u, cols, kind, engine, fn) in enumerate(units):
                w = views[n % slots]
                if u == 0 and n < AHEAD:
                    pe.wait_ge(s.started[n], 16 * starts)
                elif u == 0:
                    pe.wait_ge(s.slot_loaded[n % slots], 16 * (n // slots + (n % slots >= AHEAD)))
                if i >= 8:
                    before = units[i - 8][4]
                    pe.wait_ge(done_by[before], by_engine[before].index(i - 8) + 1)
                if kind == "token":
                    for k in range(kchunks):
                        last = nc.tensor.matmul(m.ps[i % 8][:, 0:cols], act_in[:, k, u * P:(u + 1) * P], w[:, k, 0:cols],
                                                start=(k == 0), stop=(k == kchunks - 1))
                elif cols < P:
                    for k in range(kchunks):
                        last = nc.tensor.matmul(m.ps[i % 8][0:cols, 0:T], w[:, k, 0:cols], act_in[:, k, :],
                                                start=(k == 0), stop=(k == kchunks - 1))
                else:
                    for h in range(2):
                        f = (2 * u + h) * P
                        for k in range(kchunks):
                            last = nc.tensor.matmul(m.ps[i % 8][:, h * T:(h + 1) * T], w[:, k, f:f + P], act_in[:, k, :],
                                                    start=(k == 0), stop=(k == kchunks - 1))
                last.then_inc(s.pe_done, 1)

        @block.scalar
        def _(act):
            for i in by_engine["act"]:
                act.wait_ge(s.pe_done, i + 1)
                units[i][5](view(i)).then_inc(s.act_done, 1)
            if beside is not None:
                beside[2](act)

        @block.vector
        def _(dve):
            if beside is not None:
                beside[0](dve)
            for i in by_engine["dve"]:
                dve.wait_ge(s.pe_done, i + 1)
                units[i][5](view(i)).then_inc(s.dve_done, 1)
                if beside is not None and i == XBC // 2 - 1:
                    beside[1](dve, XBC // 2)


def act_fn(nc, dst, func, scale=1.0):
    return ("act", lambda ps: nc.scalar.activation(dst, ps, func, scale=scale))


def dve_copy(nc, dst):
    return ("dve", lambda ps: nc.vector.tensor_copy(dst, ps))


def residual(nc, m, c, gates):
    def run(ps):
        for k in range(2):
            if gates is None:
                last = nc.vector.tensor_tensor(m.x_fm[:, c + k, :], ps[:, k, :], m.x_fm[:, c + k, :], ALU.add)
            else:
                last = nc.vector.scalar_tensor_tensor(out=m.x_fm[:, c + k, :], in0=ps[:, k, :], scalar=gates[:, c + k:c + k + 1],
                                                      in1=m.x_fm[:, c + k, :], op0=ALU.mult, op1=ALU.add)
        return last
    return ("dve", run)



def modulation(nc, m, stage, ada_w, c_rows, ring):
    s = m.sem
    views = [r.rearrange("p (k n) -> p k n", k=C) for r in ring]
    sums = m.arena[:, 0:6 * D].rearrange("p (g n) -> p g n", n=GROUP)
    slots = len(ring)
    loads = ada_w.shape[1] // GROUP
    per = GROUP // P
    with stage("modulation") as block:
        @block.sync
        def _(sp):
            nc.sync.dma_start(m.c_rows[:], c_rows).then_inc(s.loaded, 16)
            for n in range(AHEAD, loads):
                if n >= slots:
                    sp.wait_ge(s.dve_done, n - slots + 1)
                nc.sync.dma_start(views[n % slots], ada_w[:, n * GROUP:(n + 1) * GROUP].rearrange("(k p) n -> p k n", p=P)
                                  ).then_inc(s.slot_loaded[n % slots], 16)

        @block.tensor
        def _(pe):
            pe.wait_ge(s.loaded, 16)
            nc.tensor.transpose(m.ps[1][:, 0:C], m.c_rows[:], m.ident[0:C, 0:C]).then_inc(s.first, 1)
            for n in range(loads):
                pe.wait_ge(s.dve_done, n + 1)
                for f in range(per):
                    last = nc.tensor.matmul(m.ps[0][:, n * per + f:n * per + f + 1], sums[:, n, f * P:(f + 1) * P],
                                            m.ones[:, 0:1], start=True, stop=True)
            last.then_inc(s.pe_done, 1)

        @block.scalar
        def _(act):
            act.wait_ge(s.first, 1)
            nc.scalar.activation(m.c_act[:], m.ps[1][:, 0:C], ACT.Silu).then_inc(s.act_done, 1)

        @block.vector
        def _(dve):
            link = chain(dve, s.dve_step)
            dve.wait_ge(s.act_done, 1)
            for n in range(loads):
                if n < AHEAD:
                    dve.wait_ge(s.started[n], 16)
                else:
                    dve.wait_ge(s.slot_loaded[n % slots], 16 * (n // slots + (n % slots >= AHEAD)))
                w = views[n % slots]
                link(nc.vector.tensor_scalar(sums[:, n, :], w[:, 0, :], m.c_act[:, 0:1], None, ALU.mult))
                for k in range(1, C):
                    last = nc.vector.scalar_tensor_tensor(out=sums[:, n, :], in0=w[:, k, :], scalar=m.c_act[:, k:k + 1],
                                                          in1=sums[:, n, :], op0=ALU.mult, op1=ALU.add)
                    if k < C - 1:
                        link(last)
                last.then_inc(s.dve_done, 1)
            dve.wait_ge(s.pe_done, 1)
            nc.vector.tensor_copy(m.mod_raw[:], m.ps[0][:, 0:6 * C])


def modulation_bias(nc, m, stage, name):
    s = m.sem
    with stage(name) as block:
        @block.vector
        def _(dve):
            link = chain(dve, s.dve_step)
            link(nc.vector.tensor_tensor(m.mod[:], m.mod_raw[:], m.vecs[:, 0:6 * C], ALU.add))
            for g, sc, nv in ((0, 1, 6 * C), (1, 4, 7 * C)):
                nc.vector.scalar_tensor_tensor(out=m.gain[:, g * C:(g + 1) * C], in0=m.mod[:, sc * C:(sc + 1) * C], scalar=1.0,
                                               in1=m.vecs[:, nv:nv + C], op0=ALU.add, op1=ALU.mult)



def gmlp(nc, m, stage, ws, bs, vnorm):
    s = m.sem
    a = m.a
    with stage("gmlp") as block:
        @block.sync
        def _(sp):
            nc.sync.dma_start(a.gain_row[:], vnorm.to_broadcast([P, HEADS * HD])).then_inc(s.loaded, 16)
            nc.sync.dma_start(a.ws[:], ws.rearrange("h t s -> t h s")).then_inc(s.slot_loaded[0], 16)
            nc.sync.dma_start(a.bias_row[:], bs.rearrange("(o h) t -> o (h t)", o=1)).then_inc(s.slot_loaded[1], 16)

        @block.scalar
        def _(act):
            nc.scalar.activation(a.v_sq[:], a.v_gelu[:], ACT.Square).then_inc(s.first, 1)
            act.wait_ge(s.mean_ready, 1)
            nc.scalar.activation(a.v_root[:], a.v_mean[:], ACT.Sqrt).then_inc(s.root_ready, 1)
            for n in range(2):
                act.wait_ge(s.pe_done, n + 1)
                nc.scalar.activation(a.ws_t[:, 4 * n:4 * n + 4, :], m.ps[n][:].rearrange("p (h t) -> p h t", h=4),
                                     ACT.Copy).then_inc(s.act_done, 1)

        @block.gpsimd
        def _(pool):
            pool.wait_ge(s.act_done, 2)
            nc.gpsimd.memset(a.ws_t[HD:P, :, 0:HD], 0.0).then_inc(s.masked, 1)

        @block.tensor
        def _(pe):
            pe.wait_ge(s.slot_loaded[0], 16)
            for n in range(2):
                for k in range(4):
                    last = nc.tensor.transpose(m.ps[n][:, k * P:(k + 1) * P], a.ws[:, 4 * n + k, :], m.ident[:])
                last.then_inc(s.pe_done, 1)
            pe.wait_ge(s.slot_loaded[1], 16)
            pe.wait_ge(s.masked, 1)
            pe.wait_ge(s.normed, 1)
            for h in range(HEADS):
                lo = HD * (h % 2)
                bank = m.ps[2 + h // 2]
                for n in range(TT):
                    out = bank[lo:lo + HD, n * P:(n + 1) * P]
                    nc.tensor.matmul(out, a.v_norm[:, n, h * HD:(h + 1) * HD], a.ws_t[:, h, :], start=True, stop=False)
                    last = nc.tensor.matmul(out, m.ones[0:1, 0:HD], a.bias_row[0:1, h * P:(h + 1) * P], start=False, stop=True)
                last.then_inc(s.pe_done, 1)

        @block.vector
        def _(dve):
            link = chain(dve, s.dve_step)
            dve.wait_ge(s.first, 1)
            link(nc.vector.tensor_reduce(a.v_mean[:], a.v_sq[:].rearrange("p n (h c) -> p (n h) c", c=HD), AX_X, ALU.add))
            nc.vector.tensor_scalar(a.v_mean[:], a.v_mean[:], 1.0 / HD, EPS, ALU.mult, ALU.add).then_inc(s.mean_ready, 1)
            dve.wait_ge(s.root_ready, 1)
            link(nc.vector.reciprocal(a.v_rstd[:], a.v_root[:]))
            link(nc.vector.tensor_tensor(a.v_norm[:].rearrange("p n (h c) -> p (n h) c", c=HD),
                                         a.v_gelu[:].rearrange("p n (h c) -> p (n h) c", c=HD),
                                         a.v_rstd[:].rearrange("p (h o) -> p h o", o=1).to_broadcast([P, TT * HEADS, HD]), ALU.mult))
            dve.wait_ge(s.loaded, 16)
            nc.vector.tensor_tensor(a.v_norm[:], a.v_norm[:],
                                    a.gain_row[:].rearrange("p (o n) -> p o n", o=1).to_broadcast([P, TT, HEADS * HD]),
                                    ALU.mult).then_inc(s.normed, 1)
            for c in range(HEADS // 2):
                dve.wait_ge(s.pe_done, 2 + 2 * (c + 1))
                nc.vector.tensor_tensor(a.y[:, c, :], m.ps[2 + c][:, 0:T], a.u_gelu[:, c, :], ALU.mult)



def stick_breaking(nc, m, stage):
    s = m.sem
    a = m.a
    W3 = 3 * P
    cols = lambda x: x.rearrange("p (b t) -> p b t", b=3)
    with stage("stick") as block:
        @block.tensor
        def _(pe):
            def scores(h):
                lo, c = HD * (h % 2), h // 2
                k, q = a.k_fm[lo:lo + HD, c, :], a.q_fm[lo:lo + HD, c, :]
                if h >= 4:
                    pe.wait_ge(s.capped, h - 3)
                z = m.ps[h % 4]
                nc.tensor.matmul(z[:, 0:T], k[:, 0:P], q, start=True, stop=False, skip_group_check=True)
                nc.tensor.matmul(z[:, T:W3], k[:, P:T], q[:, P:T], start=False, stop=False,
                                 skip_group_check=True).then_inc(s.scores_ready, 1)

            def sums(h):
                pe.wait_ge(s.sp_ready, h + 1)
                z, sp = m.ps[h % 4], a.sp[:, h % 2, :]
                nc.tensor.matmul(z[:, 0:W3], m.neg_tri[:], sp, start=False, stop=False, skip_group_check=True)
                nc.tensor.matmul(z[:, P:T], m.neg_ones[:], sp[:, T:W3], start=False, stop=True,
                                 skip_group_check=True).then_inc(s.logs_ready, 1)

            def values(h):
                pe.wait_ge(s.probs_ready, h + 1)
                lo = HD * (h % 2)
                out, pr = m.ps[4 + h // 2][lo:lo + HD, :], a.probs[:, h % 2, :]
                nc.tensor.matmul(out[:, 0:T], a.v_tok[:, 0, h * HD:(h + 1) * HD], pr[:, 0:T], start=True, stop=False,
                                 skip_group_check=True)
                nc.tensor.matmul(out[:, P:T], a.v_tok[:, 1, h * HD:(h + 1) * HD], pr[:, T:W3], start=False, stop=True,
                                 skip_group_check=True).then_inc(s.values_ready, 1)

            for i in range(HEADS + 2):
                if i < HEADS:
                    scores(i)
                if 1 <= i < HEADS + 1:
                    sums(i - 1)
                if i >= 2:
                    values(i - 2)

        @block.vector
        def _(dve):
            link = chain(dve, s.dve_step)

            def softplus(h):
                dve.wait_ge(s.log_ready, h + 1)
                if h >= 2:
                    dve.wait_ge(s.logs_ready, h - 1)
                link(nc.vector.scalar_tensor_tensor(out=a.sp[:, h % 2, :], in0=m.ps[h % 4][:, 0:W3], scalar=0.0,
                                                    in1=a.lnp[:, h % 2, :], op0=ALU.max, op1=ALU.add))
                nc.vector.tensor_tensor(cols(a.sp[:, h % 2, :]), cols(a.sp[:, h % 2, :]), m.keep3[:], ALU.mult
                                        ).then_inc(s.sp_ready, 1)

            def cap(h):
                dve.wait_ge(s.logs_ready, h + 1)
                if h >= 2:
                    dve.wait_ge(s.probs_ready, h - 1)
                nc.vector.tensor_tensor(cols(a.loga[:, h % 2, :]), cols(m.ps[h % 4][:, 0:W3]), m.cap3[:], ALU.min
                                        ).then_inc(s.capped, 1)

            def out(h):
                if h % 2:
                    dve.wait_ge(s.values_ready, h + 1)
                    nc.vector.tensor_copy(a.y[:, 4 + h // 2, :], m.ps[4 + h // 2][:, 0:T])

            for i in range(HEADS + 2):
                if 1 <= i < HEADS + 1:
                    softplus(i - 1)
                if 1 <= i < HEADS + 1:
                    cap(i - 1)
                if i >= 2:
                    out(i - 2)

        @block.scalar
        def _(act):
            for i in range(HEADS + 1):
                if i < HEADS:
                    h = i
                    act.wait_ge(s.scores_ready, h + 1)
                    if h >= 2:
                        act.wait_ge(s.exp_done, h - 1)
                    nc.scalar.activation(a.absz[:, h % 2, :], m.ps[h % 4][:, 0:W3], ACT.Abs).then_inc(s.abs_ready, 1)
                    act.wait_ge(s.abs_ready, h + 1)
                    if h >= 2:
                        act.wait_ge(s.log_ready, h - 1)
                    nc.scalar.activation(a.expz[:, h % 2, :], a.absz[:, h % 2, :], ACT.Exp, scale=-1.0).then_inc(s.exp_done, 1)
                    act.wait_ge(s.exp_done, h + 1)
                    if h >= 2:
                        act.wait_ge(s.sp_ready, h - 1)
                    nc.scalar.activation(a.lnp[:, h % 2, :], a.expz[:, h % 2, :], ACT.Ln, bias=1.0).then_inc(s.log_ready, 1)
                if i >= 1:
                    h = i - 1
                    act.wait_ge(s.capped, h + 1)
                    if h >= 2:
                        act.wait_ge(s.values_ready, h - 1)
                    nc.scalar.activation(a.probs[:, h % 2, :], a.loga[:, h % 2, :], ACT.Exp).then_inc(s.probs_ready, 1)



def choose(nc, m, dve, link, t, piece):
    s = m.sem
    a = m.a
    seg = slice(2 * HEADS * t, 2 * HEADS * (t + 1))
    pair = slice(HEADS * t, HEADS * (t + 1))

    def places(values, spare, best, where, segments):
        for g in segments:
            nc.vector.max_index(out=where[:, g, 0:8], in_max=best[:, g, 0:8], in_values=values[:, g, :])
            last = nc.vector.match_replace(out=spare[:, g, :], in_to_replace=best[:, g, 0:8], in_values=values[:, g, :],
                                           imm_value=NEG)
        link(last)

    segments, pairs = range(seg.start, seg.stop), range(pair.start, pair.stop)
    if piece == 0:
        for g in segments:
            last = nc.vector.max(out=a.best[:, g, 0:8], in_=a.scores[:, g, :])
        link(last)
    elif piece in (1, 2):
        places(a.scores, a.spare, a.best, a.where, segments[(piece - 1) * HEADS:piece * HEADS])
    elif piece == 3:
        for g in segments:
            last = nc.vector.max(out=a.best[:, g, 8:16], in_=a.spare[:, g, :])
        link(last)
    elif piece == 4:
        for g in segments:
            last = nc.vector.max_index(out=a.where[:, g, 8:16], in_max=a.best[:, g, 8:16], in_values=a.spare[:, g, :])
        link(last)
        link(nc.vector.tensor_copy(a.key_no[:, seg, :], a.where[:, seg, :]))
    elif piece == 5:
        halves = a.best[:, seg, :].rearrange("p (g x) k -> p g x k", x=2)
        first = halves[:, :, 0, :].rearrange("p g (i o) -> p g i o", o=1).to_broadcast([P, HEADS, TOPK, TOPK])
        second = halves[:, :, 1, :].rearrange("p g (o j) -> p g o j", o=1).to_broadcast([P, HEADS, TOPK, TOPK])
        link(nc.vector.tensor_tensor(a.pairs[:, pair, :].rearrange("p g (i j) -> p g i j", i=TOPK), first, second, ALU.add))
        for g in pairs:
            last = nc.vector.max(out=a.top[:, g, 0:8], in_=a.pairs[:, g, :])
        link(last)
    elif piece == 6:
        places(a.pairs, a.pair_spare, a.top, a.place, pairs)
    elif piece == 7:
        for g in pairs:
            last = nc.vector.max(out=a.top[:, g, 8:16], in_=a.pair_spare[:, g, :])
        link(last)
        nc.vector.tensor_tensor(a.gate[:, pair, :], a.top[:, pair, :], a.top[:, pair, 0:1].to_broadcast([P, HEADS, TOPK]),
                                ALU.subtract).then_inc(s.abs_ready, 1)
    elif piece == 8:
        for g in pairs:
            last = nc.vector.max_index(out=a.place[:, g, 8:16], in_max=a.top[:, g, 8:16], in_values=a.pair_spare[:, g, :])
        link(last)
        nc.vector.tensor_scalar(a.place_ij[:, 0, pair, :], a.place[:, pair, :], 4, None, ALU.logical_shift_right)
        link(nc.vector.tensor_scalar(a.place_ij[:, 1, pair, :], a.place[:, pair, :], 15, None, ALU.bitwise_and))
        link(nc.vector.tensor_copy(a.place_no[:, :, pair, :], a.place_ij[:, :, pair, :]))
    elif piece in (9, 10):
        x = piece - 9
        numbers = a.key_no[:, seg, :].rearrange("p (g x) k -> p g x k", x=2)
        slots = m.count[:, 0:TOPK].rearrange("p (o k) -> p o k", o=1).to_broadcast([P, HK, TOPK])
        at = a.place_no[:, x, pair, :].rearrange("p g (k o) -> p (g k) o", o=1).to_broadcast([P, HK, TOPK])
        link(nc.vector.tensor_tensor(a.hits[:], at, slots, ALU.is_equal))
        own = numbers[:, :, x, :].rearrange("p g (o i) -> p g o i", o=1).to_broadcast([P, HEADS, TOPK, TOPK])
        hits4 = a.hits[:].rearrange("p (g k) i -> p g k i", g=HEADS)
        link(nc.vector.tensor_tensor(hits4, hits4, own, ALU.mult))
        nc.vector.tensor_reduce(a.chosen[:, x, t, :], a.hits[:], AX_X, ALU.add).then_inc(s.normed, 1)
        dve.wait_ge(s.normed, x + 1)
    elif piece == 11:
        link(nc.vector.scalar_tensor_tensor(out=a.number[:, t, :], in0=a.chosen[:, 0, t, :], scalar=float(KEYS),
                                            in1=a.chosen[:, 1, t, :], op0=ALU.mult, op1=ALU.add))
        nc.vector.tensor_scalar(m.expert[:, t, :], a.number[:, t, :], m.layer_base[:, 0:1], None, ALU.add).then_inc(s.routed, 1)
        dve.wait_ge(s.gate_exp, 1)
        link(nc.vector.tensor_reduce(a.gate_sum[:, pair], a.gate[:, pair, :], AX_X, ALU.add))
        link(nc.vector.reciprocal(a.gate_rec[:, pair], a.gate_sum[:, pair]))
        link(nc.vector.tensor_tensor(m.gate[:, t, :].rearrange("p (h k) -> p h k", k=TOPK), a.gate[:, pair, :],
                                     a.gate_rec[:, pair].rearrange("p (g o) -> p g o", o=1).to_broadcast([P, HEADS, TOPK]), ALU.mult))


PIECES = 12


def turn_keys(nc, m, pe, t):
    s = m.sem
    for x in range(2):
        pe.wait_ge(s.normed, x + 1)
        nc.tensor.transpose(m.ps[5 + x][:, 0:P], m.a.chosen[:, x, t, :], m.ident[:]).then_inc(s.keys_turned, 1)


def copy_keys(nc, m, act, t):
    s = m.sem
    pair = slice(HEADS * t, HEADS * (t + 1))
    act.wait_ge(s.abs_ready, 1)
    nc.scalar.activation(m.a.gate[:, pair, :], m.a.gate[:, pair, :], ACT.Exp).then_inc(s.gate_exp, 1)
    for x, dst, scale in ((0, m.key1_t, 1.0), (1, m.neg_key2_t, -1.0)):
        act.wait_ge(s.keys_turned, x + 1)
        nc.scalar.activation(dst[:, t * P:(t + 1) * P], m.ps[5 + x][:, 0:P], ACT.Copy, scale=scale).then_inc(s.keys_copied, 1)


def router(nc, m, stage, k1, k2):
    s = m.sem
    a = m.a
    with stage("router") as block:
        @block.sync
        def _(sp):
            nc.sync.dma_start(a.key_table[:, 0, :], k1).then_inc(s.loaded, 16)
            nc.sync.dma_start(a.key_table[:, 1, :], k2).then_inc(s.loaded, 16)

        @block.tensor
        def _(pe):
            pe.wait_ge(s.loaded, 32)
            for x in range(2):
                last = nc.tensor.transpose(m.ps[7][:, x * P:(x + 1) * P], a.key_table[:, x, :], m.ident[:])
            last.then_inc(s.first, 1)
            pe.wait_ge(s.act_done, 1)
            for n in range(8):
                t, hp = n // 4, n % 4
                for x in range(4):
                    half = x % 2
                    last = nc.tensor.matmul(m.ps[n][:, x * KEYS:(x + 1) * KEYS], a.query[:, 4 * hp + x, t * P:(t + 1) * P],
                                            a.keys_t[:, half, :], start=True, stop=True)
                last.then_inc(s.pe_done, 1)
            pe.wait_ge(s.act_done, 9)
            turn_keys(nc, m, pe, 0)

        @block.scalar
        def _(act):
            act.wait_ge(s.first, 1)
            nc.scalar.activation(a.keys_t[:], m.ps[7][:, 0:2 * P].rearrange("p (x k) -> p x k", x=2), ACT.Copy).then_inc(s.act_done, 1)
            for n in range(8):
                act.wait_ge(s.pe_done, n + 1)
                nc.scalar.activation(a.scores[:, 4 * n:4 * n + 4, :], m.ps[n][:].rearrange("p (x k) -> p x k", x=4),
                                     ACT.Copy).then_inc(s.act_done, 1)
            copy_keys(nc, m, act, 0)

        @block.vector
        def _(dve):
            link = chain(dve, s.dve_step)
            dve.wait_ge(s.act_done, 5)
            for piece in range(PIECES):
                choose(nc, m, dve, link, 0, piece)


def experts(nc, m, stage, u_table, layer):
    s = m.sem
    SUB = TOPK // GSLOTS
    QUAD = BANK // P
    QUADS = P // QUAD
    PER = TOPK // QUAD
    HOT = 2
    with stage("experts") as block:
        @block.gpsimd
        def _(pool):
            pool.sem_inc(s.slot_free, GSLOTS)
            for t in range(TT):
                if t:
                    pool.wait_ge(s.routed, t)
                with pool.Fori(0, HEADS) as h:
                    for u in range(SUB):
                        base = (t * HEADS + h) * TOPK + u * GSLOTS
                        pool.wait_ge(s.slot_free, base + 1)
                        nc.gpsimd.tensor_copy(m.index[u][:], m.expert[:, t, bass.ds(h * TOPK + u * GSLOTS, GSLOTS)]
                                              ).then_inc(s.index_ready, 1)
                        pool.wait_ge(s.index_ready, (t * HEADS + h) * SUB + u + 1)
                        for g in range(GSLOTS):
                            pool.wait_ge(s.slot_free, base + g + 1)
                            pool.sem_inc(s.gathers_started, 1)
                            nc.gpsimd.indirect_dma_start(
                                out=m.rows[g][:], out_offset=None, in_=u_table,
                                in_offset=bass.IndirectOffsetOnAxis(ap=m.index[u][:, g:g + 1], axis=0),
                            ).then_inc(s.rows_loaded[g], 16)

        @block.vector
        def _(dve):
            link = chain(dve, s.dve_step)

            def dots(t, h, u):
                for g in range(GSLOTS):
                    dve.wait_ge(s.rows_loaded[g], 16 * (((layer * TT + t) * HEADS + h) * SUB + u + 1))
                    nc.vector.scalar_tensor_tensor(out=m.rows[g][:], in0=m.rows[g][:], scalar=1.0, in1=m.h_tok[:, t, :],
                                                   op0=ALU.mult, op1=ALU.mult,
                                                   accum_out=m.dots[:, t, bass.ds(h * TOPK + u * GSLOTS + g, 1)]
                                                   ).then_inc(s.slot_free, 1)

            def weights(t):
                dve.wait_ge(s.act_done, t + 1)
                nc.vector.tensor_tensor(m.dots[:, t, :], m.dots[:, t, :], m.gate[:, t, :], ALU.mult).then_inc(s.weighted, 1)
                dve.wait_ge(s.turned, t + 1)
                link(nc.vector.tensor_copy(m.weight_t[:, t * P:(t + 1) * P], m.ps[7][:, t * P:(t + 1) * P]))

            def onehots(q, slot):
                dve.wait_ge(s.quads_placed, q + 1)
                for k in range(QUAD):
                    tok = q * QUAD + k
                    last = nc.vector.tensor_scalar(m.hot1[:, slot, k, :], m.count[:], m.key1_t[:, bass.ds(tok, 1)],
                                                   m.weight_t[:, bass.ds(tok, 1)], ALU.is_equal, ALU.mult)
                last.then_inc(s.hot_ready, 1)

            dve.sem_inc(s.quads_placed, HOT)
            for n in range(HEADS * SUB):
                dots(0, n // SUB, n % SUB)
                if n < PIECES:
                    choose(nc, m, dve, link, 1, n)
            nc.vector.tensor_scalar(m.layer_base[:], m.layer_base[:], float(EXPERTS), None, ALU.add)
            dve.wait_ge(s.keys_copied, 2)
            weights(0)
            with dve.Fori(0, HEADS) as h:
                for r in range(PER):
                    onehots(h * PER + r, r % HOT)
                    if r % 2:
                        dots(1, h, r // 2)
            weights(1)
            with dve.Fori(0, QUADS // PER) as h:
                for r in range(PER):
                    onehots(QUADS + h * PER + r, r % HOT)

        @block.scalar
        def _(act):
            def gelu(t):
                act.wait_ge(s.slot_free, GSLOTS + (t + 1) * HK)
                nc.scalar.activation(m.dots[:, t, :], m.dots[:, t, :], ACT.Gelu_apprx_tanh).then_inc(s.act_done, 1)

            def second_keys(q, made, b):
                act.wait_ge(s.second_ready, made + 1)
                act.sem_inc(s.act_waits, 1)
                for k in range(QUAD):
                    last = nc.scalar.activation(m.distance[:, b, k, :], m.count[:], ACT.Abs, bias=m.neg_key2_t[:, bass.ds(q * QUAD + k, 1)])
                last.then_inc(s.distance_ready, 1)
                act.wait_ge(s.distance_ready, made + 1)
                act.sem_inc(s.act_waits, 1)
                nc.scalar.activation(m.weights[:, :, bass.ds(q * QUAD, QUAD)], m.distance[:, b].rearrange("p k j -> p j k"),
                                     ACT.Relu, bias=1.0, scale=-1.0).then_inc(s.second_ready, 1)

            def spread(q, bank):
                act.wait_ge(s.quads_placed, HOT + q + 1)
                act.sem_inc(s.act_waits, 1)
                nc.scalar.activation(m.weights[:, :, bass.ds(q * QUAD, QUAD)],
                                     m.ps[bank][:].rearrange("p (t j) -> p j t", t=QUAD), ACT.Copy).then_inc(s.spread, 1)

            copy_keys(nc, m, act, 1)
            act.wait_ge(s.keys_copied, 2)
            gelu(0)
            act.sem_inc(s.second_ready, 2)
            act.wait_ge(s.weighted, 1)
            with act.Fori(0, QUADS // PER) as h:
                for r in range(PER):
                    q = h * PER + r
                    second_keys(q, 2 * q, 0)
                    second_keys(QUADS + q, 2 * q + 1, 1)
                    spread(q, r)
            gelu(1)
            with act.Fori(0, QUADS // PER) as h:
                for r in range(PER):
                    spread(QUADS + h * PER + r, r)

        @block.tensor
        def _(pe):
            pe.sem_inc(s.spread, PER)

            def turn(t):
                pe.wait_ge(s.weighted, t + 1)
                nc.tensor.transpose(m.ps[7][:, t * P:(t + 1) * P], m.dots[:, t, :], m.ident[:]).then_inc(s.turned, 1)

            def place(t):
                with pe.Fori(0, QUADS // PER) as h:
                    for r in range(PER):
                        q = t * QUADS + h * PER + r
                        pe.wait_ge(s.hot_ready, q + 1)
                        if t == 0:
                            pe.wait_ge(s.second_ready, 2 + 2 * q + 1)
                        pe.wait_ge(s.spread, q + 1)
                        for k in range(QUAD):
                            second = m.weights[:, :, bass.ds(q * QUAD + k, 1)].rearrange("p j o -> p (j o)")
                            last = nc.tensor.matmul(m.ps[r][:, k * KEYS:(k + 1) * KEYS], m.hot1[:, r % HOT, k, :], second,
                                                    start=True, stop=True)
                        last.then_inc(s.quads_placed, 1)

            turn_keys(nc, m, pe, 1)
            turn(0)
            place(0)
            turn(1)
            pe.wait_ge(s.second_ready, 2 + 2 * QUADS)
            place(1)


def expert_values(nc, m, stage, v_table, gates, ring, next_ada_w):
    s = m.sem
    v = v_table.rearrange("(i j) d -> i j d", i=KEYS)
    views = [r[:].rearrange("p (j d) -> p j d", j=VJ) for r in ring]
    steps = KEYS // (VJ * VSLOTS)
    SIDE = 6 * C // steps
    h, ht = m.h_fm[:].rearrange("p c t -> p (c t)"), m.h_tok[:].rearrange("p t d -> p (t d)")
    side = [x.rearrange("p (k n) -> p k n", k=C) for x in (h[:, 0:D], h[:, D:2 * D], ht[:, 0:D])]
    side_sum = [m.dots[:, 0, :], m.dots[:, 1, :], m.gate[:, 0, :]]
    with stage("values") as block:
        @block.sync
        def _(sp):
            sp.sem_inc(s.slot_free, VSLOTS)
            with sp.Fori(0, steps) as i:
                for n in range(VSLOTS):
                    sp.wait_ge(s.slot_free, i * VSLOTS + n + 1)
                    nc.sync.dma_start(views[n], v[:, bass.ds((i * VSLOTS + n) * VJ, VJ), :]).then_inc(s.slot_loaded[n], 16)

        @block.tensor
        def _(pe):
            for b in range(4):
                nc.tensor.matmul(m.ps[b][:], m.zeros_bf[:, 0:P], m.zeros_bf[:], start=True, stop=False, skip_group_check=True)
            with pe.Fori(0, steps) as i:
                for n in range(VSLOTS):
                    pe.wait_ge(s.slot_loaded[n], 16 * (i + 1))
                    for j in range(VJ):
                        for c in range(C):
                            last = nc.tensor.matmul(m.ps[c // 2][:, (c % 2) * T:(c % 2 + 1) * T], views[n][:, j, c * P:(c + 1) * P],
                                                    m.weights[:, bass.ds((i * VSLOTS + n) * VJ + j, 1), :].rearrange("p o t -> p (o t)"),
                                                    start=False, stop=False, skip_group_check=True)
                    last.then_inc(s.slot_free, 1)
                    if next_ada_w is not None and n < SIDE:
                        at = i * SIDE + n
                        pe.wait_ge(s.side_reduced, SIDE + at + 1)
                        nc.tensor.matmul(m.ps[4][:, bass.ds(at, 1)], side_sum[n], m.ones[:, 0:1], start=True, stop=True
                                         ).then_inc(s.side_summed, 1)

        if next_ada_w is not None:
            @block.scalar
            def _(act):
                with act.Fori(0, steps) as i:
                    for n in range(SIDE):
                        at = i * SIDE + n
                        act.wait_ge(s.side_reduced, at + 1)
                        nc.scalar.dma_start(side[n], next_ada_w[:, bass.ds(at * P, P)].rearrange("(k p) n -> p k n", p=P)
                                            ).then_inc(s.side_loaded[n], 16)

        @block.vector
        def _(dve):
            if next_ada_w is not None:
                dve.sem_inc(s.side_summed, SIDE)
                dve.sem_inc(s.side_reduced, SIDE)
                with dve.Fori(0, steps) as i:
                    for n in range(SIDE):
                        at = i * SIDE + n
                        dve.wait_ge(s.side_loaded[n], 16 * (i + 1))
                        nc.vector.tensor_tensor(side[n], side[n], m.c_act[:].rearrange("p (k o) -> p k o", o=1
                                                                                    ).to_broadcast([P, C, P]), ALU.mult
                                                ).then_inc(s.dve_step, 1)
                        dve.wait_ge(s.dve_step, at + 1)
                        dve.wait_ge(s.side_summed, at + 1)
                        nc.vector.tensor_reduce(side_sum[n], side[n].rearrange("p k n -> p n k"), AX_X, ALU.add
                                                ).then_inc(s.side_reduced, 1)
                dve.wait_ge(s.side_summed, SIDE + 6 * C)
                nc.vector.tensor_copy(m.mod_raw[:], m.ps[4][:, 0:6 * C])
            dve.wait_ge(s.slot_free, VSLOTS + KEYS // VJ)
            for c in range(C):
                nc.vector.scalar_tensor_tensor(out=m.x_fm[:, c, :], in0=m.ps[c // 2][:, (c % 2) * T:(c % 2 + 1) * T],
                                               scalar=gates[:, c:c + 1], in1=m.x_fm[:, c, :], op0=ALU.mult, op1=ALU.add)



def convolution(nc, m):
    s = m.sem
    a = m.a

    def pad(dve):
        nc.vector.memset(a.xbc[:, :, 0:CONV - 1], 0.0).then_inc(s.dve_step, 1)

    def taps(dve, evacuated):
        dve.wait_ge(s.dve_step, 1)
        dve.wait_ge(s.dve_done, evacuated)
        for k in range(CONV):
            for c in range(XBC):
                tap = m.vecs[:, m.v_conv + k * XBC + c:m.v_conv + k * XBC + c + 1]
                x = a.xbc[:, c, k:k + T]
                if k == 0:
                    last = nc.vector.tensor_scalar(a.conv[:, c, :], x, tap, None, ALU.mult)
                else:
                    last = nc.vector.scalar_tensor_tensor(out=a.conv[:, c, :], in0=x, scalar=tap, in1=a.conv[:, c, :],
                                                          op0=ALU.mult, op1=ALU.add)
                if k == CONV - 1:
                    last.then_inc(s.scaled, 1)
            if k < CONV - 1:
                last.then_inc(s.dve_step, 1)
                dve.wait_ge(s.dve_step, k + 2)

    def silu(act):
        for c in range(XBC):
            act.wait_ge(s.scaled, c + 1)
            nc.scalar.activation(a.conv[:, c, :], a.conv[:, c, :], ACT.Silu,
                                 bias=m.vecs[:, m.v_conv_b + c:m.v_conv_b + c + 1])
    return pad, taps, silu


def ssd(nc, m, stage, a_log, dt_bias, d_skip):
    s = m.sem
    a = m.a
    W3 = 3 * P
    with stage("ssd_prepare") as block:
        @block.sync
        def _(sp):
            row = lambda x: x.to_broadcast([P, SSD_HEADS])
            nc.sync.dma_start(a.a_row[:], row(a_log)).then_inc(s.loaded, 16)
            nc.sync.dma_start(a.dt_row[:], row(dt_bias)).then_inc(s.loaded, 16)
            for x in range(2):
                nc.sync.dma_start(a.d_col[HD * x:HD * (x + 1), :],
                                  d_skip.rearrange("o (c x) -> o c x", x=2)[:, :, x].to_broadcast([HD, C]),
                                  allow_slow_non_contiguous=True).then_inc(s.loaded, 16)
            sp.wait_ge(s.loaded, 64)

        @block.tensor
        def _(pe):
            for n in range(4):
                t, q = n // 2, n % 2
                for k in range(4):
                    last = nc.tensor.transpose(m.ps[n][:, k * P:(k + 1) * P], a.conv[:, 4 * q + k, t * P:(t + 1) * P], m.ident[:])
                last.then_inc(s.pe_done, 1)
            for g in range(2):
                b, c = a.conv[HD * g:HD * (g + 1), 8, :], a.conv[HD * g:HD * (g + 1), 9, :]
                nc.tensor.matmul(m.ps[4 + g][:, 0:T], b[:, 0:P], c, start=True, stop=False, skip_group_check=True)
                nc.tensor.matmul(m.ps[4 + g][:, T:W3], b[:, P:T], c[:, P:T], start=False, stop=True,
                                 skip_group_check=True).then_inc(s.pe_done, 1)

        @block.vector
        def _(dve):
            link = chain(dve, s.dve_step)
            dve.wait_ge(s.loaded, 64)
            link(nc.vector.tensor_tensor(a.dt[:], a.dt_raw[:], a.dt_row[:].rearrange("p (o h) -> p o h", o=1
                                                                                 ).to_broadcast([P, TT, SSD_HEADS]), ALU.add))
            nc.vector.scalar_tensor_tensor(out=a.dt_abs[:], in0=a.dt[:], scalar=-1.0, in1=a.dt[:], op0=ALU.mult, op1=ALU.max).then_inc(s.abs_ready, 1)
            for n in range(4):
                t, q = n // 2, n % 2
                dve.wait_ge(s.pe_done, n + 1)
                nc.vector.tensor_copy(a.xs_tok[:, t, q * BANK:(q + 1) * BANK], m.ps[n][:])
            for g in range(2):
                dve.wait_ge(s.pe_done, 5 + g)
                nc.vector.tensor_tensor(a.cb[:, g, :].rearrange("p (b i) -> p b i", b=3),
                                        m.ps[4 + g][:, 0:W3].rearrange("p (b i) -> p b i", b=3), m.upto3[:], ALU.mult)
            dve.wait_ge(s.act_done, 3)
            link(nc.vector.scalar_tensor_tensor(out=a.dt[:], in0=a.dt[:], scalar=0.0, in1=a.dt_ln[:], op0=ALU.max, op1=ALU.add))
            nc.vector.scalar_tensor_tensor(out=a.dta[:], in0=a.dt[:], scalar=-1.0,
                                           in1=a.a_exp[:].rearrange("p (o h) -> p o h", o=1).to_broadcast([P, TT, SSD_HEADS]),
                                           op0=ALU.mult, op1=ALU.mult)

        @block.scalar
        def _(act):
            act.wait_ge(s.loaded, 64)
            nc.scalar.activation(a.a_exp[:], a.a_row[:], ACT.Exp).then_inc(s.act_done, 1)
            act.wait_ge(s.abs_ready, 1)
            nc.scalar.activation(a.dt_exp[:], a.dt_abs[:], ACT.Exp, scale=-1.0).then_inc(s.act_done, 1)
            act.wait_ge(s.act_done, 2)
            nc.scalar.activation(a.dt_ln[:], a.dt_exp[:], ACT.Ln, bias=1.0).then_inc(s.act_done, 1)

    with stage("ssd") as block:
        @block.vector
        def _(dve):
            def steps(h):
                if h >= 2:
                    dve.wait_ge(s.scores_ready, h - 1)
                b = h % 2
                nc.vector.tensor_scalar(a.steps[:, b, 0, :], m.after[:], a.dta[:, 0, h:h + 1], None, ALU.mult)
                nc.vector.tensor_scalar(a.steps[:, b, 1, :], m.after[:], a.dta[:, 1, h:h + 1], None, ALU.mult)
                nc.vector.tensor_scalar(a.steps[:, b, 2, :], m.ones[:], a.dta[:, 1, h:h + 1], None, ALU.mult
                                        ).then_inc(s.sp_ready, 1)

            def mix(h):
                dve.wait_ge(s.exp_done, h + 1)
                if h >= 2:
                    dve.wait_ge(s.values_ready, h - 1)
                g = h // (SSD_HEADS // 2)
                nc.vector.scalar_tensor_tensor(out=a.mix[:, h % 2, 0:T], in0=a.decay[:, h % 2, 0:T], scalar=a.dt[:, 0, h:h + 1],
                                               in1=a.cb[:, g, 0:T], op0=ALU.mult, op1=ALU.mult)
                nc.vector.scalar_tensor_tensor(out=a.mix[:, h % 2, T:W3], in0=a.decay[:, h % 2, T:W3], scalar=a.dt[:, 1, h:h + 1],
                                               in1=a.cb[:, g, T:W3], op0=ALU.mult, op1=ALU.mult).then_inc(s.probs_ready, 1)

            def out(c):
                dve.wait_ge(s.values_ready, 2 * c + 2)
                nc.vector.scalar_tensor_tensor(out=a.ya[:, c, :], in0=a.conv[:, c, :], scalar=a.d_col[:, c:c + 1],
                                               in1=m.ps[4 + c % 4][:, 0:T], op0=ALU.mult, op1=ALU.add).then_inc(s.dve_done, 1)
                dve.wait_ge(s.dve_done, c + 1)
                nc.vector.tensor_tensor(a.ya[:, c, :], a.ya[:, c, :], a.z_silu[:, c, :], ALU.mult)

            for i in range(SSD_HEADS + 3):
                if i < SSD_HEADS:
                    steps(i)
                if 1 <= i < SSD_HEADS + 1:
                    mix(i - 1)
                if i >= 3 and (i - 3) % 2:
                    out((i - 3) // 2)

        @block.tensor
        def _(pe):
            def sums(h):
                pe.wait_ge(s.sp_ready, h + 1)
                if h >= 4:
                    pe.wait_ge(s.exp_done, h - 3)
                b, seg = h % 2, m.ps[h % 4]
                upto = m.upto3[:].rearrange("p b i -> p (b i)")
                nc.tensor.matmul(seg[:, 0:T], a.steps[:, b, 0, :], upto[:, 0:T], start=True, stop=False, skip_group_check=True)
                nc.tensor.matmul(seg[:, P:T], a.steps[:, b, 2, :], upto[:, 0:P], start=False, stop=False, skip_group_check=True)
                nc.tensor.matmul(seg[:, T:W3], a.steps[:, b, 1, :], upto[:, 0:P], start=False, stop=True,
                                 skip_group_check=True).then_inc(s.scores_ready, 1)

            def products(h):
                pe.wait_ge(s.probs_ready, h + 1)
                if h >= 8:
                    pe.wait_ge(s.dve_done, h // 2 - 3)
                lo = HD * (h % 2)
                out = m.ps[4 + (h // 2) % 4][lo:lo + HD, :]
                nc.tensor.matmul(out[:, 0:T], a.xs_tok[:, 0, h * HD:(h + 1) * HD], a.mix[:, h % 2, 0:T], start=True, stop=False,
                                 skip_group_check=True)
                nc.tensor.matmul(out[:, P:T], a.xs_tok[:, 1, h * HD:(h + 1) * HD], a.mix[:, h % 2, T:W3], start=False, stop=True,
                                 skip_group_check=True).then_inc(s.values_ready, 1)

            for i in range(SSD_HEADS + 1):
                if i < SSD_HEADS:
                    sums(i)
                if i >= 1:
                    products(i - 1)

        @block.scalar
        def _(act):
            for h in range(SSD_HEADS):
                act.wait_ge(s.scores_ready, h + 1)
                if h >= 2:
                    act.wait_ge(s.probs_ready, h - 1)
                nc.scalar.activation(a.decay[:, h % 2, :], m.ps[h % 4][:, 0:W3], ACT.Exp).then_inc(s.exp_done, 1)



def gla(nc, m, stage, gate_w2):
    s = m.sem
    a = m.a
    NC = T // GLA_CHUNK
    F4 = 4
    chunks = lambda x: x.rearrange("p f (n t) -> p (f n) t", t=GLA_CHUNK)
    wide = lambda col: col.to_broadcast([P, F4 * NC, GLA_CHUNK])
    with stage("gla_decays") as block:
        @block.sync
        def _(sp):
            nc.sync.dma_start(a.w2[:], gate_w2).then_inc(s.loaded, 16)

        @block.gpsimd
        def _(pool):
            nc.gpsimd.memset(a.carry[:], 1.0).then_inc(s.first, 1)
            pool.wait_ge(s.first, 1)
            nc.gpsimd.memset(a.carry[:].rearrange("p (n t) -> p n t", t=GLA_CHUNK)[:, :, 0:1], 0.0).then_inc(s.masked, 1)

        @block.tensor
        def _(pe):
            pe.wait_ge(s.loaded, 16)
            for f in range(F4):
                last = nc.tensor.matmul(m.ps[f // 2][:, (f % 2) * T:(f % 2 + 1) * T], a.w2[:, f * P:(f + 1) * P], a.lr[:],
                                        start=True, stop=True)
            last.then_inc(s.pe_done, 1)
            for n in range(2):
                pe.wait_ge(s.weighted, 1)
                for f in range(F4):
                    last = nc.tensor.transpose(m.ps[2 + n][:, f * P:(f + 1) * P], a.k_end[:, f, n * P:(n + 1) * P], m.ident[:])
                last.then_inc(s.turned, 1)

        @block.vector
        def _(dve):
            link = chain(dve, s.dve_step)
            dve.wait_ge(s.pe_done, 1)
            for f in range(F4):
                link(nc.vector.tensor_scalar(a.gl[:, f, :], m.ps[f // 2][:, (f % 2) * T:(f % 2 + 1) * T],
                                             m.vecs[:, m.v_gate_b + f:m.v_gate_b + f + 1], None, ALU.add))
            nc.vector.scalar_tensor_tensor(out=a.g_abs[:], in0=a.gl[:], scalar=-1.0, in1=a.gl[:], op0=ALU.mult, op1=ALU.max).then_inc(s.abs_ready, 1)
            dve.wait_ge(s.log_ready, 1)
            link(nc.vector.scalar_tensor_tensor(out=a.gl[:], in0=a.gl[:], scalar=0.0, in1=a.g_ln[:], op0=ALU.min, op1=ALU.subtract))
            link(nc.vector.tensor_scalar(a.gl[:], a.gl[:], 1.0 / GLA_NORMALIZER, None, ALU.mult))
            dve.wait_ge(s.masked, 1)
            for f in range(F4):
                last = nc.vector.tensor_tensor_scan(a.gcs[:, f, :], a.carry[:], a.gl[:, f, :], 0.0, ALU.mult, ALU.add)
            link(last)
            g = chunks(a.gcs[:])
            mid, end = g[:, :, GLA_CHUNK // 2:GLA_CHUNK // 2 + 1], g[:, :, GLA_CHUNK - 1:GLA_CHUNK]
            nc.vector.tensor_tensor(chunks(a.to_mid[:]), g, wide(mid), ALU.subtract).then_inc(s.dve_done, 1)
            nc.vector.tensor_tensor(chunks(a.to_end[:]), g, wide(end), ALU.subtract).then_inc(s.dve_done, 1)
            for e, dst, x in ((1, a.q_mid, a.q_fm), (2, a.k_mid, a.k_fm), (3, a.q_start, a.q_fm), (4, a.k_end, a.k_fm)):
                dve.wait_ge(s.exp_done, e)
                last = nc.vector.tensor_tensor(dst[:], dst[:], x[:], ALU.mult)
            last.then_inc(s.weighted, 1)
            for n in range(2):
                dve.wait_ge(s.turned, n + 1)
                nc.vector.tensor_copy(a.k_end_tok[:, n, :], m.ps[2 + n][:])

        @block.scalar
        def _(act):
            act.wait_ge(s.abs_ready, 1)
            nc.scalar.activation(a.g_exp[:], a.g_abs[:], ACT.Exp, scale=-1.0).then_inc(s.act_done, 1)
            act.wait_ge(s.act_done, 1)
            nc.scalar.activation(a.g_ln[:], a.g_exp[:], ACT.Ln, bias=1.0).then_inc(s.log_ready, 1)
            act.wait_ge(s.dve_done, 1)
            nc.scalar.activation(a.q_mid[:], a.to_mid[:], ACT.Exp).then_inc(s.exp_done, 1)
            nc.scalar.activation(a.k_mid[:], a.to_mid[:], ACT.Exp, scale=-1.0).then_inc(s.exp_done, 1)
            nc.scalar.activation(a.q_start[:], a.gcs[:], ACT.Exp).then_inc(s.exp_done, 1)
            act.wait_ge(s.dve_done, 2)
            nc.scalar.activation(a.k_end[:], a.to_end[:], ACT.Exp, scale=-1.0).then_inc(s.exp_done, 1)
            nc.scalar.activation(a.g_chunk[:], chunks(a.gcs[:])[:, :, GLA_CHUNK - 1:GLA_CHUNK].rearrange("p g o -> p (g o)"), ACT.Exp)

    with stage("gla_states") as block:
        @block.tensor
        def _(pe):
            for n in range(NC - 1):
                r = slice(GLA_CHUNK * (n % 2), GLA_CHUNK * (n % 2 + 1))
                if n >= 2:
                    pe.wait_ge(s.dve_done, F4 * (n - 1))
                for f in range(F4):
                    bank = m.ps[4 * (n % 2) + f]
                    for x in range(2):
                        h = 2 * f + x
                        last = nc.tensor.matmul(bank[HD * x:HD * (x + 1), 0:P],
                                                a.k_end_tok[r, n // 2, h * HD:(h + 1) * HD], a.v_tok[r, n // 2, h * P:(h + 1) * P],
                                                start=True, stop=True)
                    last.then_inc(s.pe_done, 1)

        @block.vector
        def _(dve):
            for n in range(NC - 1):
                for f in range(F4):
                    dve.wait_ge(s.pe_done, n * F4 + f + 1)
                    own = m.ps[4 * (n % 2) + f][:, 0:P]
                    if n == 0:
                        nc.vector.tensor_copy(a.state[:, 1, f, :], own).then_inc(s.dve_done, 1)
                    else:
                        dve.wait_ge(s.dve_done, (n - 1) * F4 + f + 1)
                        nc.vector.scalar_tensor_tensor(out=a.state[:, n + 1, f, :], in0=a.state[:, n, f, :],
                                                       scalar=a.g_chunk[:, f * NC + n:f * NC + n + 1], in1=own,
                                                       op0=ALU.mult, op1=ALU.add).then_inc(s.dve_done, 1)

    with stage("gla_out") as block:
        @block.tensor
        def _(pe):
            def scores(h):
                lo, f = HD * (h % 2), h // 2
                if h >= 2:
                    pe.wait_ge(s.masked, h - 1)
                for n in range(NC):
                    t = slice(n * GLA_CHUNK, (n + 1) * GLA_CHUNK)
                    last = nc.tensor.matmul(m.ps[h % 2][GLA_CHUNK * (n % 2):GLA_CHUNK * (n % 2 + 1), (n // 2) * GLA_CHUNK:(n // 2 + 1) * GLA_CHUNK],
                                            a.k_mid[lo:lo + HD, f, t], a.q_mid[lo:lo + HD, f, t], start=True, stop=True)
                last.then_inc(s.scores_ready, 1)

            def out(h):
                lo, f = HD * (h % 2), h // 2
                pe.wait_ge(s.masked, h + 1)
                if h >= 3:
                    pe.wait_ge(s.dve_done, h - 2)
                for n in range(NC):
                    r = slice(GLA_CHUNK * (n % 2), GLA_CHUNK * (n % 2 + 1))
                    t = slice(n * GLA_CHUNK, (n + 1) * GLA_CHUNK)
                    same = n % 2 == h % 2
                    main, other = m.ps[2 + 2 * (h % 3)][:, t], m.ps[3 + 2 * (h % 3)][:, t]
                    last = nc.tensor.matmul(main if same else other, a.v_tok[r, n // 2, h * P:(h + 1) * P],
                                            a.intra[r, h % 2, n // 2, :], start=True, stop=not (same and n))
                    if n:
                        last = nc.tensor.matmul(main, a.state[lo:lo + HD, n, f, :], a.q_start[lo:lo + HD, f, t],
                                                start=not same, stop=True)
                last.then_inc(s.values_ready, 1)

            for i in range(HEADS + 1):
                if i < HEADS:
                    scores(i)
                if i >= 1:
                    out(i - 1)

        @block.vector
        def _(dve):
            def mask(h):
                dve.wait_ge(s.scores_ready, h + 1)
                if h >= 2:
                    dve.wait_ge(s.values_ready, h - 1)
                for x in range(2):
                    r = slice(GLA_CHUNK * x, GLA_CHUNK * (x + 1))
                    upto = m.upto3[r, 0:1, GLA_CHUNK * x:GLA_CHUNK * (x + 1)].to_broadcast([GLA_CHUNK, 2, GLA_CHUNK])
                    last = nc.vector.tensor_tensor(a.intra[r, h % 2, :, :],
                                                   m.ps[h % 2][r, 0:2 * GLA_CHUNK].rearrange("p (n i) -> p n i", n=2), upto, ALU.mult)
                last.then_inc(s.masked, 1)

            def out(h):
                dve.wait_ge(s.act_done, h + 1)
                main, other = a.ob[:, h, :], m.ps[3 + 2 * (h % 3)]
                part = lambda n: slice(n * GLA_CHUNK, (n + 1) * GLA_CHUNK)
                if h % 2:
                    nc.vector.tensor_copy(main[:, part(0)], other[:, part(0)])
                    last = nc.vector.tensor_tensor(main[:, part(2)], main[:, part(2)], other[:, part(2)], ALU.add)
                else:
                    nc.vector.tensor_tensor(main[:, part(1)], main[:, part(1)], other[:, part(1)], ALU.add)
                    last = nc.vector.tensor_tensor(main[:, part(3)], main[:, part(3)], other[:, part(3)], ALU.add)
                last.then_inc(s.dve_done, 1)

            for i in range(HEADS + 1):
                if i < HEADS:
                    mask(i)
                if i >= 1:
                    out(i - 1)

        @block.scalar
        def _(act):
            for h in range(HEADS):
                act.wait_ge(s.values_ready, h + 1)
                first = GLA_CHUNK * (h % 2)
                nc.scalar.activation(a.ob[:, h, first:T], m.ps[2 + 2 * (h % 3)][:, first:T], ACT.Copy).then_inc(s.act_done, 1)


def multiply(nc, m, stage, name, dst, other):
    with stage(name) as block:
        @block.vector
        def _(dve):
            nc.vector.tensor_tensor(dst[:], dst[:], other[:], ALU.mult)



def moba(nc, m, stage, ahead):
    s = m.sem
    a = m.a
    units = [(h, t) for h in range(MOBA_HEADS) for t in range(TT)]
    N = len(units)
    with stage("moba") as block:
        @block.sync
        def _(sp):
            start_loads(nc, m, ahead)

        @block.tensor
        def _(pe):
            def scores(u):
                h, t = units[u]
                lo, c = HD * (h % 2), h // 2
                if u >= 4:
                    pe.wait_ge(s.capped, u - 3)
                keys = (t + 1) * P
                nc.tensor.matmul(m.ps[u % 4][:, 0:keys], a.mq[lo:lo + HD, c, t * P:(t + 1) * P], a.mk[lo:lo + HD, c, 0:keys],
                                 start=True, stop=True).then_inc(s.scores_ready, 1)

            def turn(u):
                h, t = units[u]
                pe.wait_ge(s.weighted, u + 1)
                if u >= 2:
                    pe.wait_ge(s.turned, u - 1)
                for k in range(t + 1):
                    last = nc.tensor.transpose(m.ps[4 + u % 2][:, k * P:(k + 1) * P], a.mp[:, u % 4, k * P:(k + 1) * P], m.ident[:])
                last.then_inc(s.pe_done, 1)

            def values(u):
                h, t = units[u]
                pe.wait_ge(s.turned, u + 1)
                lo, bank = HD * (h % 2), m.ps[6 + (h // 2) % 2]
                if h >= 4 and h % 2 == 0 and t == 0:
                    pe.wait_ge(s.dve_done, h // 2 - 1)
                for k in range(t + 1):
                    last = nc.tensor.matmul(bank[lo:lo + HD, t * P:(t + 1) * P], a.mv[:, k, h * HD:(h + 1) * HD],
                                            a.mp_t[:, u % 2, k * P:(k + 1) * P], start=(k == 0), stop=(k == t))
                last.then_inc(s.values_ready, 1)

            for i in range(N + 3):
                if i < N:
                    scores(i)
                if 2 <= i < N + 2:
                    turn(i - 2)
                if i >= 3:
                    values(i - 3)

        @block.vector
        def _(dve):
            link = chain(dve, s.dve_step)

            def cap(u):
                h, t = units[u]
                keys = (t + 1) * P
                dve.wait_ge(s.scores_ready, u + 1)
                if u >= 2:
                    dve.wait_ge(s.exp_done, u - 1)
                diag = slice(t * P, keys)
                if t:
                    nc.vector.tensor_copy(a.ms[:, u % 2, 0:P], m.ps[u % 4][:, 0:P])
                link(nc.vector.tensor_tensor(a.ms[:, u % 2, diag], m.ps[u % 4][:, diag], a.causal[:], ALU.min))
                nc.vector.tensor_reduce(a.neg_max[:, u:u + 1], a.ms[:, u % 2, 0:keys], AX_X, ALU.max, negate=True
                                        ).then_inc(s.capped, 1)

            def weigh(u):
                h, t = units[u]
                keys = (t + 1) * P
                dve.wait_ge(s.exp_done, u + 1)
                link(nc.vector.reciprocal(a.rec[:, u:u + 1], a.sums[:, u:u + 1]))
                nc.vector.tensor_scalar(a.mp[:, u % 4, 0:keys], a.mp[:, u % 4, 0:keys], a.rec[:, u:u + 1], None, ALU.mult
                                        ).then_inc(s.weighted, 1)

            def out(c):
                dve.wait_ge(s.values_ready, 4 * (c + 1))
                nc.vector.tensor_tensor(a.my[:, c, :], m.ps[6 + c % 2][:, 0:T], a.mz[:, c, :], ALU.mult).then_inc(s.dve_done, 1)

            for i in range(N + 4):
                if i < N:
                    cap(i)
                if 1 <= i < N + 1:
                    weigh(i - 1)
                if i >= 4 and (i - 4) % 4 == 3:
                    out((i - 4) // 4)

        @block.scalar
        def _(act):
            def exps(u):
                h, t = units[u]
                keys = (t + 1) * P
                act.wait_ge(s.capped, u + 1)
                if u >= 4:
                    act.wait_ge(s.pe_done, u - 3)
                nc.scalar.activation(a.mp[:, u % 4, 0:keys], a.ms[:, u % 2, 0:keys], ACT.Exp, bias=a.neg_max[:, u:u + 1],
                                     accum_out=a.sums[:, u:u + 1]).then_inc(s.exp_done, 1)

            def copy(u):
                h, t = units[u]
                keys = (t + 1) * P
                act.wait_ge(s.pe_done, u + 1)
                if u >= 2:
                    act.wait_ge(s.values_ready, u - 1)
                nc.scalar.activation(a.mp_t[:, u % 2, 0:keys], m.ps[4 + u % 2][:, 0:keys], ACT.Copy).then_inc(s.turned, 1)

            for i in range(N + 2):
                if i < N:
                    exps(i)
                if i >= 2:
                    copy(i - 2)



def allocate(nc, ctx):
    m = Names()

    def sb(name, shape, dt=F32):
        return ctx.enter_context(nc.sbuf_tensor(name, shape, dt))

    m.ps = [ctx.enter_context(nc.psum_tensor(f"bank{i}", [P, BANK], F32)) for i in range(8)]
    m.x_fm = sb("x_fm", [P, C, T])
    m.h_fm = sb("h_fm", [P, C, T])
    m.h_tok = sb("h_tok", [P, TT, D])
    m.x_tok = m.h_tok
    m.dots = sb("dots", [P, TT, HK])
    m.gate = sb("gate", [P, TT, HK])
    m.expert = sb("expert", [P, TT, HK], U32)
    m.key1_t = sb("key1_t", [P, T])
    m.neg_key2_t = sb("neg_key2_t", [P, T])
    m.weight_t = sb("weight_t", [P, T])
    m.index = [sb(f"index{u}", [P, GSLOTS], U32) for u in range(TOPK // GSLOTS)]
    m.layer_base = sb("layer_base", [P, 1])
    m.ident = sb("ident", [P, P])
    m.ones = sb("ones", [P, P])
    m.neg_ones = sb("neg_ones", [P, P])
    m.neg_tri = sb("neg_tri", [P, P])
    m.after = sb("after", [P, P])
    m.count = sb("count", [P, P])
    m.keep3 = sb("keep3", [P, 3, P])
    m.cap3 = sb("cap3", [P, 3, P])
    m.upto3 = sb("upto3", [P, 3, P])
    m.zeros_bf = sb("zeros_bf", [P, BANK], BF16)
    m.vec_rows = sb("vec_rows", [P, P])
    m.vecs = sb("vecs", [P, P])
    m.mod = sb("mod", [P, 6 * C])
    m.mod_raw = sb("mod_raw", [P, 6 * C])
    m.gain = sb("gain", [P, 2 * C])
    m.c_rows = sb("c_rows", [C, P])
    m.c_act = sb("c_act", [P, C])

    hot = m.h_fm[:].rearrange("p c t -> p (c t)")
    m.hot1 = hot[:, 0:D].rearrange("p (b k i) -> p b k i", b=2, k=4)
    m.distance = hot[:, D:2 * D].rearrange("p (b k j) -> p b k j", b=2, k=4)

    m.stream = sb("stream", [P, GSLOTS * D])
    m.rows = [m.stream[:, g * D:(g + 1) * D] for g in range(GSLOTS)]
    m.value_ring = [m.stream[:, n * VJ * D:(n + 1) * VJ * D] for n in range(VSLOTS)]
    part = lambda n: m.stream[:, n * C * T:(n + 1) * C * T].rearrange("p (c t) -> p c t", c=C)
    m.squares, m.mean, m.root, m.rstd = (part(n) for n in range(4))

    m.arena = sb("arena", [P, KEYS * T])
    m.weights = m.arena[:].rearrange("p (j t) -> p j t", j=KEYS)
    slot = 8 * GROUP
    end = KEYS * T
    m.weight_ring = [m.arena[:, end - slot:end], m.arena[:, end - 2 * slot:end - slot], m.stream[:, 0:slot], m.stream[:, slot:2 * slot]]
    m.arena_end = end - 2 * slot

    sems = ["loaded", "stored", "slot_free", "pe_done", "act_done", "dve_done", "first", "masked", "normed", "dve_step",
            "pool_step", "mean_ready", "root_ready", "scaled", "scores_ready", "capped", "sp_ready", "logs_ready", "probs_ready",
            "values_ready", "abs_ready", "exp_done", "log_ready", "index_ready", "weighted", "turned", "quads_placed",
            "hot_ready", "spread", "gathers_started",
            "routed", "gate_exp", "keys_turned", "keys_copied", "distance_ready", "second_ready", "act_waits",
            "side_summed", "side_reduced"]
    named = {name: nc.alloc_semaphore(name) for name in sems}
    handles = list(named.values())
    m.sem = Names(**named)
    m.sem.slot_loaded = [nc.alloc_semaphore(f"slot_loaded{g}") for g in range(GSLOTS)]
    m.sem.side_loaded = m.sem.slot_loaded[VSLOTS:]
    handles += m.sem.slot_loaded
    nums = sorted(h.num for h in handles)
    assert nums == list(range(nums[0], nums[-1] + 1))
    m.to_clear = range(nums[0], nums[-1] + 1)
    m.sem.started = [nc.alloc_semaphore(f"started{n}") for n in range(AHEAD)]
    m.starts = 0
    m.sem.rows_loaded = [nc.alloc_semaphore(f"rows_loaded{g}") for g in range(GSLOTS)]
    return m


def carve(m, plan):
    views = {}
    at = 0
    for name, (shape, dt) in plan.items():
        size = 1
        for n in shape:
            size *= n
        assert at + size <= m.arena_end, name
        v = m.arena[:, at:at + size]
        at += size
        if dt is not F32:
            v = v.bitcast(dt)
        if len(shape) == 2:
            v = v.rearrange("p (a b) -> p a b", a=shape[0])
        elif len(shape) == 3:
            v = v.rearrange("p (a b c) -> p a b c", a=shape[0], b=shape[1])
        views[name] = v
    return Names(**views)


def columns(w, start, count):
    return w[:, start:start + count]


def rows_of(v):
    return v.rearrange("(r p) -> r p", p=P)


def first_block(nc, m, stage, d, layer):
    at = lambda name: d[name][layer:layer + 1]
    one = lambda name, pattern, **k: at(name).rearrange(pattern, **k)
    load_vectors(nc, m, stage, "vectors1", [
        (one("ada_b", "l (r p) -> (l r) p", p=P), 6 * C), (one("norm_mix", "l (r p) -> (l r) p", p=P), C),
        (one("norm_ffn", "l (r p) -> (l r) p", p=P), C), (one("out_norm_a", "l (r p) -> (l r) p", p=P), 4),
        (one("out_norm_b", "l (r p) -> (l r) p", p=P), 4)], m.vecs)
    if layer == 0:
        modulation(nc, m, stage, one("ada_w", "l k n -> (l k) n"), d["c"].rearrange("o (r p) -> (o r) p", p=P), m.weight_ring)
    modulation_bias(nc, m, stage, "modulation_bias")
    chunk = lambda i: m.mod[:, i * C:(i + 1) * C]

    w_in, w_out, w_q = (one(n, "l k n -> (l k) n") for n in ("w_in", "w_out", "peer_wq"))
    groups = lambda w, order: [columns(w, n * GROUP, GROUP) for n in order]
    norm(nc, m, stage, "norm1", m.x_fm, m.h_fm, C, m.gain[:, 0:C], chunk(0), ahead=groups(w_in, (0, 1)))
    a = m.a = carve(m, {
        "y": ([C, T], F32), "u_gelu": ([4, T], F32), "v_gelu": ([TT, 512], F32), "q_fm": ([4, T], F32), "k_fm": ([4, T], F32),
        "v_tok": ([TT, 512], F32), "v_sq": ([TT, 512], F32), "v_norm": ([TT, 512], F32), "gain_row": ([512], F32),
        "ws": ([HEADS, P], F32), "ws_t": ([HEADS, P], F32), "bias_row": ([HEADS * P], F32),
        "v_mean": ([16], F32), "v_root": ([16], F32), "v_rstd": ([16], F32),
        "absz": ([2, 384], F32), "expz": ([2, 384], F32), "lnp": ([2, 384], F32), "sp": ([2, 384], F32),
        "loga": ([2, 384], F32), "probs": ([2, 384], F32)})
    a.bias_row = a.bias_row[0:1, :]
    w = w_in
    G = GROUP
    project(nc, m, stage, "in1", m.h_fm, C, [
        (columns(w, 0, G), "feature", [act_fn(nc, a.u_gelu[:, 2 * u:2 * u + 2, :], ACT.Gelu_apprx_tanh) for u in range(2)]),
        (columns(w, G, G), "token", [act_fn(nc, a.v_gelu[:, t, :], ACT.Gelu_apprx_tanh) for t in range(2)]),
        (columns(w, 2 * G, G), "feature", [act_fn(nc, a.q_fm[:, 2 * u:2 * u + 2, :], ACT.Copy, scale=HD ** -0.5) for u in range(2)]),
        (columns(w, 3 * G, G), "feature", [dve_copy(nc, a.k_fm[:, 2 * u:2 * u + 2, :]) for u in range(2)]),
        (columns(w, 4 * G, G), "token", [dve_copy(nc, a.v_tok[:, t, :]) for t in range(2)])], m.weight_ring)
    gmlp(nc, m, stage, one("gm_ws", "l h t s -> (l h) t s"), one("gm_bs", "l h t -> (l h) t"), at("gm_vnorm"))
    stick_breaking(nc, m, stage)
    norm(nc, m, stage, "norm_y", a.y, m.h_fm, C, m.vecs[:, 8 * C:9 * C], width=4, ahead=groups(w_out, (0, 1)))
    w = w_out
    project(nc, m, stage, "out1", m.h_fm, C, [
        (columns(w, n * G, G), "feature", [residual(nc, m, 4 * n + 2 * u, chunk(2)) for u in range(2)]) for n in range(2)], m.weight_ring)

    norm(nc, m, stage, "norm2", m.x_fm, m.h_fm, C, m.gain[:, C:2 * C], chunk(3), ahead=groups(w_q, (0, 1)))
    to_token_major(nc, m, stage, "h_token", m.h_fm, m.h_tok)
    a = m.a = carve(m, {
        "query": ([2 * C, T], F32), "key_table": ([2, P], F32), "keys_t": ([2, P], F32),
        "scores": ([32, KEYS], F32), "spare": ([32, KEYS], F32), "best": ([32, TOPK], F32), "where": ([32, TOPK], U32),
        "key_no": ([32, TOPK], F32), "top": ([16, TOPK], F32), "place": ([16, TOPK], U32),
        "place_ij": ([2, 16, TOPK], U32), "place_no": ([2, 16, TOPK], F32), "gate": ([16, TOPK], F32),
        "gate_sum": ([16], F32), "gate_rec": ([16], F32), "chosen": ([2, TT, HK], F32), "number": ([TT, HK], F32),
        "hits": ([HK, TOPK], F32), "pairs": ([16, 256], F32)})
    a.pair_spare = a.scores.rearrange("p a b -> p (a b)").rearrange("p (g n) -> p g n", g=16)
    w = w_q
    project(nc, m, stage, "query", m.h_fm, C, [
        (columns(w, n * G, G), "feature",
         [(act_fn(nc, a.query[:, 4 * n + 2 * u:4 * n + 2 * u + 2, :], ACT.Copy) if u else
           dve_copy(nc, a.query[:, 4 * n + 2 * u:4 * n + 2 * u + 2, :])) for u in range(2)]) for n in range(4)], m.weight_ring)
    router(nc, m, stage, one("peer_k1", "l k n -> (l k) n"), one("peer_k2", "l k n -> (l k) n"))
    experts(nc, m, stage, d["peer_u"].rearrange("l e n -> (l e) n"), layer)
    expert_values(nc, m, stage, one("peer_v", "l e n -> (l e) n"), chunk(5), m.value_ring,
                  d["ada_w"][layer + 1] if layer + 1 < DEPTH else None)


def second_block(nc, m, stage, d, out):
    flat = lambda name: d[name].rearrange("l n -> (l n)")
    m.v_norm, m.v_conv, m.v_conv_b, m.v_ssd, m.v_gate_b, m.v_gla, m.v_odd, m.v_final = 0, 8, 48, 58, 66, 70, 78, 86
    load_vectors(nc, m, stage, "vectors2", [
        (rows_of(flat("even_norm_2")), 8), (d["even_conv_w_2"].rearrange("l k (r p) -> (l k r) p", p=P), 40),
        (rows_of(flat("even_conv_b_2")), 10), (rows_of(flat("even_ssd_norm_2")), 8), (rows_of(flat("even_gate_b_2")), 4),
        (d["even_gla_norm_2"].to_broadcast([8, P]), 8), (rows_of(flat("odd_norm_2")), 8), (rows_of(d["final_norm_2"]), 8)], m.vecs)
    vec = lambda start, n=C: m.vecs[:, start:start + n]

    w = d["even_w_in_2"].rearrange("l k n -> (l k) n")
    o_x, o_dt, o_q, o_k, o_v, o_lr, o_g = 1024, 2304, 2320, 2832, 3344, 4368, 4384
    norm(nc, m, stage, "norm3", m.x_fm, m.h_fm, C, vec(m.v_norm), ahead=[columns(w, o_x, GROUP), columns(w, o_x + GROUP, GROUP)])
    a = m.a = carve(m, {
        "z_silu": ([C, T], F32), "xbc": ([XBC, T + CONV - 1], F32), "q_fm": ([4, T], F32), "k_fm": ([4, T], F32),
        "v_tok": ([TT, D], F32), "g_silu": ([C, T], F32), "lr": ([T], F32), "dt_raw": ([TT, SSD_HEADS], F32),
        "conv": ([XBC, T], F32),
        "dt_row": ([16], F32), "a_row": ([16], F32), "a_exp": ([16], F32), "d_col": ([C], F32),
        "dt": ([TT, 16], F32), "dt_abs": ([TT, 16], F32), "dt_exp": ([TT, 16], F32), "dt_ln": ([TT, 16], F32), "dta": ([TT, 16], F32),
        "work": ([8800], F32)})
    work, at = a.work, [0]

    def take(*shape):
        size = 1
        for n in shape:
            size *= n
        v = work[:, at[0]:at[0] + size]
        at[0] += size
        assert at[0] <= 8800
        if len(shape) == 2:
            return v.rearrange("p (a b) -> p a b", a=shape[0])
        if len(shape) == 3:
            return v.rearrange("p (a b c) -> p a b c", a=shape[0], b=shape[1])
        return v

    y = m.h_tok[:].rearrange("p t d -> p (t d)").rearrange("p (c t) -> p c t", c=C)
    a.ya = y
    a.xs_tok, a.cb = take(TT, D), take(2, 384)
    a.steps, a.decay, a.mix = take(2, 3, P), take(2, 384), take(2, 384)
    a.lr = a.lr[0:16, :]
    G = GROUP
    xbc = lambda c: a.xbc[:, c:c + 2, CONV - 1:]
    project(nc, m, stage, "in2", m.h_fm, C, [
        (columns(w, o_x + n * G, G if n < 2 else 256), "feature", [dve_copy(nc, xbc(4 * n + 2 * u)) for u in range(2 if n < 2 else 1)])
        for n in range(3)] + [
        (columns(w, n * G, G), "feature", [act_fn(nc, a.z_silu[:, 4 * n + 2 * u:4 * n + 2 * u + 2, :], ACT.Silu) for u in range(2)])
        for n in range(2)] + [
        (columns(w, o_dt, 16), "token", [dve_copy(nc, a.dt_raw[:, t, :]) for t in range(2)]),
        (columns(w, o_q, G), "feature", [act_fn(nc, a.q_fm[:, 2 * u:2 * u + 2, :], ACT.Copy, scale=HD ** -0.5) for u in range(2)]),
        (columns(w, o_k, G), "feature", [dve_copy(nc, a.k_fm[:, 2 * u:2 * u + 2, :]) for u in range(2)]),
        (columns(w, o_v, G), "token", [dve_copy(nc, a.v_tok[:, t, 0:G]) for t in range(2)]),
        (columns(w, o_v + G, G), "token", [dve_copy(nc, a.v_tok[:, t, G:2 * G]) for t in range(2)]),
        (columns(w, o_lr, 16), "feature", [dve_copy(nc, a.lr[:, :])])] + [
        (columns(w, o_g + n * G, G), "feature", [act_fn(nc, a.g_silu[:, 4 * n + 2 * u:4 * n + 2 * u + 2, :], ACT.Silu) for u in range(2)])
        for n in range(2)], m.weight_ring, beside=convolution(nc, m))
    ssd(nc, m, stage, d["even_a_log_2"], d["even_dt_bias_2"], d["even_d_skip_2"])
    norm(nc, m, stage, "norm_ssd", a.ya, m.h_fm, C, vec(m.v_ssd))

    at[0] = 0
    a.gl, a.gcs, a.q_mid, a.k_mid, a.q_start, a.k_end = (take(4, T) for _ in range(6))
    a.k_end_tok = take(TT, 512)
    a.g_chunk, a.carry = take(16), take(T)
    a.w2 = take(512)[0:16, :]
    a.intra = take(2, 2, GLA_CHUNK)
    free = m.arena[:, 0:4600]
    piece = lambda n: free[:, n * 1024:(n + 1) * 1024].rearrange("p (f t) -> p f t", f=4)
    a.to_mid, a.to_end, a.g_ln, a.g_exp = (piece(n) for n in range(4))
    a.g_abs = a.to_mid
    a.state = a.conv.rearrange("p c t -> p (c t)")[:, 0:4 * 512].rearrange("p (n f v) -> p n f v", n=4, f=4)
    a.ob = y
    gla(nc, m, stage, d["even_gate_w2_2"].rearrange("l r n -> (l r) n"))
    w = d["even_w_out_2"].rearrange("l k n -> (l k) n")
    norm(nc, m, stage, "norm_gla", a.ob, a.ob, C, vec(m.v_gla), width=1, ahead=[columns(w, n * 256, 256) for n in range(2)])
    multiply(nc, m, stage, "gate_gla", a.ob, a.g_silu)
    both = TwoHalves(m.h_fm, a.ob)
    project(nc, m, stage, "out2", both, 2 * C, [
        (columns(w, n * 256, 256), "feature", [residual(nc, m, 2 * n, None)]) for n in range(4)], m.weight_ring)

    w = d["odd_w_in_2"].rearrange("l k n -> (l k) n")
    norm(nc, m, stage, "norm4", m.x_fm, m.h_fm, C, vec(m.v_odd), ahead=[columns(w, n * G, G) for n in range(2)])
    a = m.a = carve(m, {
        "mq": ([C, T], F32), "mk": ([C, T], F32), "mv": ([TT, D], F32), "mz": ([C, T], F32), "my": ([C, T], F32),
        "ms": ([2, T], F32), "mp": ([4, T], F32), "mp_t": ([2, T], F32), "neg_max": ([32], F32), "sums": ([32], F32),
        "rec": ([32], F32), "causal": ([P], F32)})
    project(nc, m, stage, "in3", m.h_fm, C, [
        (columns(w, n * G, G), "feature", [act_fn(nc, a.mq[:, 4 * n + 2 * u:4 * n + 2 * u + 2, :], ACT.Copy, scale=HD ** -0.5) for u in range(2)])
        for n in range(2)] + [
        (columns(w, D + n * G, G), "feature", [dve_copy(nc, a.mk[:, 4 * n + 2 * u:4 * n + 2 * u + 2, :]) for u in range(2)])
        for n in range(2)] + [
        (columns(w, 2 * D + n * G, G), "token", [dve_copy(nc, a.mv[:, t, n * G:(n + 1) * G]) for t in range(2)])
        for n in range(2)] + [
        (columns(w, 3 * D + n * G, G), "feature", [act_fn(nc, a.mz[:, 4 * n + 2 * u:4 * n + 2 * u + 2, :], ACT.Silu) for u in range(2)])
        for n in range(2)], m.weight_ring)
    causal_mask(nc, m, stage)
    w = d["odd_w_out_2"].rearrange("l k n -> (l k) n")
    moba(nc, m, stage, [columns(w, n * G, G) for n in range(2)])
    project(nc, m, stage, "out3", a.my, C, [
        (columns(w, n * G, G), "feature", [residual(nc, m, 4 * n + 2 * u, None) for u in range(2)]) for n in range(2)], m.weight_ring)
    norm(nc, m, stage, "norm5", m.x_fm, m.h_fm, C, vec(m.v_final))
    to_token_major(nc, m, stage, "out_token", m.h_fm, m.h_tok, store=out.rearrange("o t d -> (o t) d"))


class TwoHalves:

    def __init__(self, first, second):
        self.parts = (first, second)

    def __getitem__(self, key):
        p, k, t = key
        return self.parts[k // C][p, k % C, t]


def causal_mask(nc, m, stage):
    s = m.sem
    with stage("causal") as block:
        @block.gpsimd
        def _(pool):
            nc.gpsimd.memset(m.a.causal[:], -NEG).then_inc(s.first, 1)
            pool.wait_ge(s.first, 1)
            nc.gpsimd.affine_select(out=m.a.causal[:], in_=m.a.causal[:], compare_op=ALU.is_ge, fill=-1.0e30,
                                    base=0, pattern=[[-1, P]], channel_multiplier=1)


def program(nc, d, out):
    with ExitStack() as ctx:
        m = allocate(nc, ctx)
        m.x_dram = d["x"]
        stage = stage_maker(nc, m.to_clear)
        make_constants(nc, m, stage, [columns(d["ada_w"][0], n * GROUP, GROUP) for n in range(AHEAD)])
        to_feature_major(nc, m, stage, "x_feature", m.x_tok, m.x_fm)
        for layer in range(DEPTH):
            first_block(nc, m, stage_maker(nc, m.to_clear, f"_{layer}"), d, layer)
        load_vectors(nc, m, stage, "vectors_final", [(rows_of(d["final_norm"]), C)], m.vecs)
        norm(nc, m, stage, "norm_final", m.x_fm, m.x_fm, C, m.vecs[:, 0:C])
        second_block(nc, m, stage, d, out)


_INS = ["x", "c", "ada_w", "ada_b", "norm_mix", "norm_ffn", "w_in", "gm_ws", "gm_bs", "gm_vnorm", "out_norm_a", "out_norm_b",
        "w_out", "peer_wq", "peer_k1", "peer_k2", "peer_u", "peer_v", "final_norm", "even_norm_2", "even_w_in_2",
        "even_conv_w_2", "even_conv_b_2", "even_a_log_2", "even_dt_bias_2", "even_d_skip_2", "even_ssd_norm_2",
        "even_gate_w2_2", "even_gate_b_2", "even_gla_norm_2", "even_w_out_2", "odd_norm_2", "odd_w_in_2", "odd_w_out_2",
        "final_norm_2"]


def kernel(**inputs):
    import numpy as np
    import concourse.bacc as bacc
    from concourse.bass_utils import run_bass_kernel_spmd

    nc = bacc.Bacc("TRN2", target_bir_lowering=False, num_devices=1)
    arrays, d = {}, {}
    for name in _INS:
        x = np.ascontiguousarray(inputs[name])
        arrays[f"in_{name}"] = x
        d[name] = nc.dram_tensor(f"in_{name}", x.shape, mybir.dt.from_np(x.dtype), kind="ExternalInput").ap()
    out = nc.dram_tensor("out", (1, T, D), F32, kind="ExternalOutput").ap()
    program(nc, d, out)
    r = run_bass_kernel_spmd(nc, [arrays], core_ids=[0])
    return r.results[0]["out"]
```
